# Optimizing a Trainium2 kernel written in Bass

```python
import math
import jax, jax.numpy as jnp
from jax import lax
import numpy as np

D_MODEL = 1024
BATCH = 1
SEQ = 128
DEPTH = 1
DEC_BATCH = 1
DEC_SEQ = 512
PAST_LEN = 128

GRID_W = 64
EPS = 1e-6
N_MLSTM_HEADS = 4
MLSTM_HEAD_DIM = D_MODEL // 8
MLSTM_WIDTH = N_MLSTM_HEADS * MLSTM_HEAD_DIM
MLSTM_CHUNK = 128
FORGET_BIAS = 3.0
N_GATES = 4 * N_MLSTM_HEADS
N_DIFF_HEADS = 4
DIFF_QK_DIM = D_MODEL // 16
DIFF_V_DIM = 2 * DIFF_QK_DIM
DIFF_WIDTH = N_DIFF_HEADS * DIFF_V_DIM
DIFF_QK_WIDTH = N_DIFF_HEADS * 2 * DIFF_QK_DIM
Q_BLOCK = 128
ROPE_THETA = 10000.0
MIX_WIDTH = MLSTM_WIDTH + DIFF_WIDTH
OFF_MQ = 0
OFF_MK = OFF_MQ + MLSTM_WIDTH
OFF_MV = OFF_MK + MLSTM_WIDTH
OFF_MO = OFF_MV + MLSTM_WIDTH
OFF_GATE = OFF_MO + MLSTM_WIDTH
OFF_DQ = OFF_GATE + N_GATES
OFF_DK = OFF_DQ + DIFF_QK_WIDTH
OFF_DV = OFF_DK + DIFF_QK_WIDTH
IN_WIDTH = OFF_DV + DIFF_WIDTH
N_GROUPS = 4
EXPERTS_PER_GROUP = 4
N_EXPERTS = N_GROUPS * EXPERTS_PER_GROUP
TOP_K_IN_GROUP = 2
EXPERT_HIDDEN = D_MODEL // 4

kernel_name = 'hymba_mlstm_diffattn_hmoe_diffusion_step'

def rmsnorm(x, g):
    x32 = x.astype(jnp.float32)
    y = x32 * lax.rsqrt(jnp.mean(x32 * x32, axis=-1, keepdims=True) + EPS)
    return (y * g.astype(jnp.float32)).astype(x.dtype)

def head_rmsnorm(x):
    x32 = x.astype(jnp.float32)
    return (x32 * lax.rsqrt(jnp.mean(x32 * x32, axis=-1, keepdims=True) + EPS)).astype(x.dtype)

def ada_mod(cvec, w_ada, b_ada):
    m = jax.nn.silu(cvec) @ w_ada + b_ada
    return jnp.split(m[:, None, :], 6, axis=-1)

def project(h, w_in, b_gate):
    B, S, _ = h.shape
    p = h @ w_in
    q_m = p[..., OFF_MQ:OFF_MK].reshape(B, S, N_MLSTM_HEADS, MLSTM_HEAD_DIM)
    k_m = p[..., OFF_MK:OFF_MV].reshape(B, S, N_MLSTM_HEADS, MLSTM_HEAD_DIM) * (MLSTM_HEAD_DIM ** -0.5)
    v_m = p[..., OFF_MV:OFF_MO].reshape(B, S, N_MLSTM_HEADS, MLSTM_HEAD_DIM)
    o_m = p[..., OFF_MO:OFF_GATE]
    gates = (p[..., OFF_GATE:OFF_DQ].astype(jnp.float32) + b_gate.astype(jnp.float32)).reshape(B, S, 4, N_MLSTM_HEADS)
    q_d = p[..., OFF_DQ:OFF_DK].reshape(B, S, N_DIFF_HEADS, 2, DIFF_QK_DIM)
    k_d = p[..., OFF_DK:OFF_DV].reshape(B, S, N_DIFF_HEADS, 2, DIFF_QK_DIM)
    v_d = p[..., OFF_DV:IN_WIDTH].reshape(B, S, N_DIFF_HEADS, DIFF_V_DIM)
    return q_m, k_m, v_m, o_m, gates, q_d, k_d, v_d

def rope_1d(x, pos):
    half = x.shape[-1] // 2
    freqs = ROPE_THETA ** (-jnp.arange(half, dtype=jnp.float32) / half)
    ang = pos.astype(jnp.float32)[:, None] * freqs[None, :]
    cos = jnp.cos(ang)[None, :, None, None, :]
    sin = jnp.sin(ang)[None, :, None, None, :]
    x32 = x.astype(jnp.float32)
    x1, x2 = x32[..., :half], x32[..., half:]
    return jnp.concatenate([x1 * cos - x2 * sin, x1 * sin + x2 * cos], axis=-1).astype(x.dtype)

def axial_rope(x):
    S = x.shape[1]
    n_rows = S // GRID_W
    row = jnp.repeat(jnp.arange(n_rows), GRID_W)
    col = jnp.tile(jnp.arange(GRID_W), n_rows)
    half = x.shape[-1] // 2
    return jnp.concatenate([rope_1d(x[..., :half], row), rope_1d(x[..., half:], col)], axis=-1)

def diff_lambda_value(lp, lam_init):
    lp = lp.astype(jnp.float32)
    return jnp.exp(jnp.sum(lp[0] * lp[1])) - jnp.exp(jnp.sum(lp[2] * lp[3])) + lam_init

def diff_attention_block(q, k, v, lam):
    s = jnp.einsum('bqhmd,bkhmd->bhmqk', q, k).astype(jnp.float32) * (DIFF_QK_DIM ** -0.5)
    p = jax.nn.softmax(s, axis=-1)
    a = p[:, :, 0] - lam * p[:, :, 1]
    return jnp.einsum('bhqk,bkhd->bqhd', a.astype(v.dtype), v)

def blocked_diff_attention(q, k, v, lam):
    B, S, H, _, d = q.shape
    nb = S // Q_BLOCK
    qb = q.reshape(B, nb, Q_BLOCK, H, 2, d).swapaxes(0, 1)
    out = lax.map(lambda qi: diff_attention_block(qi, k, v, lam), qb)
    return out.swapaxes(0, 1).reshape(B, S, H, v.shape[-1])

def mlstm_chunk_scan(q, k, v, i_pre, f_pre, C0, n0, m0):
    B, S, H, d = q.shape
    nc = S // MLSTM_CHUNK
    f32 = jnp.float32

    def chunks(t):
        return t.reshape((B, nc, MLSTM_CHUNK) + t.shape[2:]).swapaxes(0, 1)

    xs = (chunks(q), chunks(k), chunks(v), chunks(i_pre.astype(f32)),
          chunks(jax.nn.log_sigmoid(f_pre.astype(f32))))
    causal = jnp.tril(jnp.ones((MLSTM_CHUNK, MLSTM_CHUNK), dtype=bool))

    def step(carry, inp):
        C, n, m = carry
        qc, kc, vc, ic, lfc = inp
        qc, kc, vc = qc.astype(f32), kc.astype(f32), vc.astype(f32)
        b = jnp.cumsum(lfc, axis=1).swapaxes(1, 2)
        ig = ic.swapaxes(1, 2)
        dmat = jnp.where(causal, b[..., :, None] - b[..., None, :] + ig[..., None, :], -jnp.inf)
        inter = b + m[..., None]
        m_t = jnp.maximum(inter, jnp.max(dmat, axis=-1))
        w_intra = jnp.exp(dmat - m_t[..., None])
        w_state = jnp.exp(inter - m_t)
        s = jnp.einsum('blhd,bshd->bhls', qc, kc) * w_intra
        num = jnp.einsum('bhls,bshd->bhld', s, vc) + w_state[..., None] * jnp.einsum('bhvk,blhk->bhlv', C, qc)
        den = jnp.sum(s, axis=-1) + w_state * jnp.einsum('bhk,blhk->bhl', n, qc)
        h = num / jnp.maximum(jnp.abs(den), jnp.exp(-m_t))[..., None]
        b_last = b[..., -1]
        g = b_last[..., None] - b + ig
        m_new = jnp.maximum(b_last + m, jnp.max(g, axis=-1))
        w_k = jnp.exp(g - m_new[..., None])
        decay = jnp.exp(b_last + m - m_new)
        C_new = decay[..., None, None] * C + jnp.einsum('bhs,bshv,bshk->bhvk', w_k, vc, kc)
        n_new = decay[..., None] * n + jnp.einsum('bhs,bshk->bhk', w_k, kc)
        return (C_new, n_new, m_new), h.swapaxes(1, 2)

    (C, n, m), hs = lax.scan(step, (C0.astype(f32), n0.astype(f32), m0.astype(f32)), xs)
    return hs.swapaxes(0, 1).reshape(B, S, H, d).astype(q.dtype), C, n, m

def mlstm_bidirectional(q, k, v, gates, C0, n0, m0):
    rev = lambda t: jnp.flip(t, axis=1)
    h_f, C_f, n_f, m_f = mlstm_chunk_scan(q, k, v, gates[:, :, 0], gates[:, :, 1], C0[:, 0], n0[:, 0], m0[:, 0])
    h_b, C_b, n_b, m_b = mlstm_chunk_scan(rev(q), rev(k), rev(v), rev(gates[:, :, 2]), rev(gates[:, :, 3]),
                                          C0[:, 1], n0[:, 1], m0[:, 1])
    h = h_f + rev(h_b)
    return h, jnp.stack([C_f, C_b], axis=1), jnp.stack([n_f, n_b], axis=1), jnp.stack([m_f, m_b], axis=1)

def mix_output(h_m, o_m, h_d, lam_init, g_m, g_d, w_out):
    B, S = h_m.shape[:2]
    hm = head_rmsnorm(h_m).reshape(B, S, MLSTM_WIDTH) * g_m * jax.nn.sigmoid(o_m)
    hd = head_rmsnorm(h_d).reshape(B, S, DIFF_WIDTH) * g_d * (1.0 - lam_init)
    return jnp.concatenate([hm, hd], axis=-1) @ w_out

def hierarchical_moe(h, w_rg, b_rg, w_re, b_re, w_gu, w_dn):
    B, S, D = h.shape
    x = h.reshape(B * S, D)
    f32 = jnp.float32
    lg = (x @ w_rg).astype(f32) + b_rg.astype(f32)
    pg = jax.nn.softmax(lg, axis=-1)
    grp = jnp.argmax(lg, axis=-1)
    p_grp = jnp.max(pg, axis=-1, keepdims=True)
    le = ((x @ w_re).astype(f32) + b_re.astype(f32)).reshape(B * S, N_GROUPS, EXPERTS_PER_GROUP)
    le_sel = jnp.einsum('nge,ng->ne', le, jax.nn.one_hot(grp, N_GROUPS, dtype=f32))
    pe = jax.nn.softmax(le_sel, axis=-1)
    top_p, top_i = lax.top_k(pe, TOP_K_IN_GROUP)
    top_p = top_p / jnp.sum(top_p, axis=-1, keepdims=True)
    expert_idx = grp[:, None] * EXPERTS_PER_GROUP + top_i
    comb = jnp.sum(jax.nn.one_hot(expert_idx, N_EXPERTS, dtype=f32) * (top_p * p_grp)[..., None], axis=1).astype(x.dtype)
    y = jnp.zeros_like(x)
    for e in range(N_EXPERTS):
        a, u = jnp.split(x @ w_gu[e], 2, axis=-1)
        y = y + comb[:, e:e + 1] * ((jax.nn.silu(a) * u) @ w_dn[e])
    return y.reshape(B, S, D)

def setup_inputs(seed: int = 0) -> dict:
    key = jax.random.key(seed)
    ks = jax.random.split(key, 32)
    f32 = jnp.float32
    D = D_MODEL

    def nrm(k, shape, s):
        return s * jax.random.normal(k, shape, f32)

    gate_noise = nrm(ks[14], (DEPTH, 4, N_MLSTM_HEADS), 0.3)
    gate_base = jnp.array([0.0, FORGET_BIAS, 0.0, FORGET_BIAS], f32)[None, :, None]
    return {
        'x_prompt': nrm(ks[0], (BATCH, SEQ, D), 1.0),
        'x_sample': nrm(ks[1], (DEC_BATCH, DEC_SEQ, D), 1.0),
        'cache_k': nrm(ks[2], (DEC_BATCH, DEPTH, PAST_LEN, N_DIFF_HEADS, 2, DIFF_QK_DIM), 1.0),
        'cache_v': nrm(ks[3], (DEC_BATCH, DEPTH, PAST_LEN, N_DIFF_HEADS, DIFF_V_DIM), 1.0),
        'state_C': nrm(ks[4], (DEC_BATCH, DEPTH, 2, N_MLSTM_HEADS, MLSTM_HEAD_DIM, MLSTM_HEAD_DIM), 0.1),
        'state_n': nrm(ks[5], (DEC_BATCH, DEPTH, 2, N_MLSTM_HEADS, MLSTM_HEAD_DIM), 0.3),
        'state_m': nrm(ks[6], (DEC_BATCH, DEPTH, 2, N_MLSTM_HEADS), 1.0),
        'c': nrm(ks[7], (DEC_BATCH, D), 1.0),
        'c_ctx': nrm(ks[8], (D,), 1.0),
        'w_ada': nrm(ks[9], (DEPTH, D, 6 * D), 0.5 * D ** -0.5),
        'b_ada': nrm(ks[10], (DEPTH, 6 * D), 0.01),
        'norm_mix': 1.0 + nrm(ks[11], (DEPTH, D), 0.01),
        'norm_ffn': 1.0 + nrm(ks[12], (DEPTH, D), 0.01),
        'w_in': nrm(ks[13], (DEPTH, D, IN_WIDTH), D ** -0.5),
        'b_gate': (gate_noise + gate_base).reshape(DEPTH, N_GATES),
        'mlstm_norm': 1.0 + nrm(ks[15], (DEPTH, MLSTM_WIDTH), 0.01),
        'diff_norm': 1.0 + nrm(ks[16], (DEPTH, DIFF_WIDTH), 0.01),
        'diff_lambda': nrm(ks[17], (DEPTH, 4, DIFF_QK_DIM), 0.1),
        'w_out': nrm(ks[18], (DEPTH, MIX_WIDTH, D), MIX_WIDTH ** -0.5),
        'w_route_group': nrm(ks[19], (DEPTH, D, N_GROUPS), D ** -0.5),
        'b_route_group': nrm(ks[20], (DEPTH, N_GROUPS), 0.01),
        'w_route_expert': nrm(ks[21], (DEPTH, D, N_EXPERTS), D ** -0.5),
        'b_route_expert': nrm(ks[22], (DEPTH, N_EXPERTS), 0.01),
        'w_gate_up': nrm(ks[23], (DEPTH, N_EXPERTS, D, 2 * EXPERT_HIDDEN), D ** -0.5),
        'w_down': nrm(ks[24], (DEPTH, N_EXPERTS, EXPERT_HIDDEN, D), EXPERT_HIDDEN ** -0.5),
        'final_norm': 1.0 + nrm(ks[25], (D,), 0.01),
    }

def reference(x_prompt, x_sample, cache_k, cache_v, state_C, state_n, state_m, c, c_ctx,
              w_ada, b_ada, norm_mix, norm_ffn, w_in, b_gate, mlstm_norm, diff_norm, diff_lambda, w_out,
              w_route_group, b_route_group, w_route_expert, b_route_expert, w_gate_up, w_down, final_norm):
    xp = x_prompt
    xs = x_sample
    Bp = xp.shape[0]
    new_k, new_v, new_C, new_n, new_m = [], [], [], [], []
    for l in range(DEPTH):
        lam_init = 0.8 - 0.6 * math.exp(-0.3 * l)
        lam = diff_lambda_value(diff_lambda[l], lam_init)
        moe_w = (w_route_group[l], b_route_group[l], w_route_expert[l], b_route_expert[l], w_gate_up[l], w_down[l])

        sh1, sc1, g1, sh2, sc2, g2 = ada_mod(c_ctx[None, :], w_ada[l], b_ada[l])
        h = rmsnorm(xp, norm_mix[l]) * (1.0 + sc1) + sh1
        q_m, k_m, v_m, o_m, gates, q_d, k_d, v_d = project(h, w_in[l], b_gate[l])
        zC = jnp.zeros((Bp, 2, N_MLSTM_HEADS, MLSTM_HEAD_DIM, MLSTM_HEAD_DIM), jnp.float32)
        zn = jnp.zeros((Bp, 2, N_MLSTM_HEADS, MLSTM_HEAD_DIM), jnp.float32)
        zm = jnp.zeros((Bp, 2, N_MLSTM_HEADS), jnp.float32)
        h_m, C_ctx, n_ctx, m_ctx = mlstm_bidirectional(q_m, k_m, v_m, gates, zC, zn, zm)
        h_d = blocked_diff_attention(q_d, k_d, v_d, lam)
        xp = xp + g1 * mix_output(h_m, o_m, h_d, lam_init, mlstm_norm[l], diff_norm[l], w_out[l])
        h = rmsnorm(xp, norm_ffn[l]) * (1.0 + sc2) + sh2
        xp = xp + g2 * hierarchical_moe(h, *moe_w)
        new_k.append(k_d)
        new_v.append(v_d)
        new_C.append(C_ctx)
        new_n.append(n_ctx)
        new_m.append(m_ctx)

        sh1, sc1, g1, sh2, sc2, g2 = ada_mod(c, w_ada[l], b_ada[l])
        h = rmsnorm(xs, norm_mix[l]) * (1.0 + sc1) + sh1
        q_m, k_m, v_m, o_m, gates, q_d, k_d, v_d = project(h, w_in[l], b_gate[l])
        h_m, _, _, _ = mlstm_bidirectional(q_m, k_m, v_m, gates, state_C[:, l], state_n[:, l], state_m[:, l])
        q_r = axial_rope(q_d)
        k_all = jnp.concatenate([axial_rope(k_d), cache_k[:, l].astype(k_d.dtype)], axis=1)
        v_all = jnp.concatenate([v_d, cache_v[:, l].astype(v_d.dtype)], axis=1)
        h_d = blocked_diff_attention(q_r, k_all, v_all, lam)
        xs = xs + g1 * mix_output(h_m, o_m, h_d, lam_init, mlstm_norm[l], diff_norm[l], w_out[l])
        h = rmsnorm(xs, norm_ffn[l]) * (1.0 + sc2) + sh2
        xs = xs + g2 * hierarchical_moe(h, *moe_w)

    y_prompt = rmsnorm(xp, final_norm)
    y_sample = rmsnorm(xs, final_norm)
    return (y_prompt, y_sample, jnp.stack(new_k, axis=1), jnp.stack(new_v, axis=1),
            jnp.stack(new_C, axis=1), jnp.stack(new_n, axis=1), jnp.stack(new_m, axis=1))


_drawn_inputs = setup_inputs


def setup_inputs(seed=0):
    import zlib

    import numpy as np

    out = dict(_drawn_inputs(seed))
    spreads = {}
    factors = {'state_C': 7.648,
     'state_n': 7.52,
     'state_m': 8.0,
     'norm_mix': 3.062,
     'norm_ffn': 7.36,
     'mlstm_norm': 8.0,
     'diff_norm': 8.0,
     'diff_lambda': 6.899,
     'b_route_group': 8.0,
     'b_route_expert': 8.0,
     'final_norm': 31.344,
     'cache_k': 8.0,
     'cache_v': 8.0}
    for name, (base, spread) in spreads.items():
        noise = np.random.default_rng([zlib.crc32(name.encode()), seed]).standard_normal(out[name].shape)
        drawn = base * np.exp(spread * noise) if base else spread * noise
        out[name] = __import__('jax').numpy.asarray(drawn.astype(out[name].dtype))
    for name, factor in factors.items():
        out[name] = (out[name] * factor).astype(out[name].dtype)
    return out
```

```python
import math
from contextlib import ExitStack

import numpy as np

import concourse.bass as bass
from concourse import mybir

F32 = mybir.dt.float32
BF16 = mybir.dt.bfloat16
U32 = mybir.dt.uint32
I32 = mybir.dt.int32
ALU = mybir.AluOpType
ACT = mybir.ActivationFunctionType
AX = mybir.AxisListType

P = 128
D = 1024
KD = D // P
CTX = 128
LAT = 512
T = CTX + LAT
NT = T // P
PAST = 128
H = 4
HD = 128
QK = 64
EPS = 1e-6
GRID_W = 64
THETA = 10000.0
LAM_INIT = 0.8 - 0.6 * math.exp(0.0)
OFF = {"mq": 0, "mk": 512, "mv": 1024, "mo": 1536, "gate": 2048, "dq": 2064, "dk": 2576, "dv": 3088}
NG = 4
EG = 4
NE = NG * EG
EH = D // 4
ROUNDS = T // P
BIG = 2.0 ** 99
WIN_ORDER = ["mk", "mq", "mv", "mo", "dk", "dq", "dv"]
SMALL = 16
CHUNKS = ([("ada", n * 512) for n in range(4)] + [(w, OFF[w]) for w in WIN_ORDER]
          + [("ada", n * 512) for n in range(4, 12)] + [("out", 0), ("out", 512)])
ADA1, WIN0, ADA2, WOUT = 0, 4, 11, 19


def shape_constants():
    ident = np.eye(P, dtype=np.float32)
    s, t = np.arange(P)[:, None], np.arange(P)[None, :]
    masks = np.stack([np.where(s > t, BIG, 0.0), np.where(s < t, BIG, 0.0),
                      np.where(s < t, 1.0, 0.0), np.ones((P, P))], 1).astype(np.float32)
    sel = np.zeros((H, H, P), np.float32)
    for h in range(H):
        sel[h, h] = 1.0
    eye4 = np.tile(np.eye(H, dtype=np.float32)[:, None, :], (1, NT, 1))
    half = QK // 4
    freqs = THETA ** (-np.arange(half, dtype=np.float32) / half)
    tok = np.arange(LAT)
    ang = np.stack([(tok // GRID_W)[:, None] * freqs, (tok % GRID_W)[:, None] * freqs], 1).astype(np.float32)
    cos = np.stack([np.cos(ang), np.cos(ang)], 2)
    sin = np.stack([-np.sin(ang), np.sin(ang)], 2)
    rope = np.stack([cos, sin], 0).reshape(2, LAT // P, P, QK).transpose(2, 0, 1, 3).astype(np.float32)
    misc = np.zeros((P, 64), np.float32)
    misc[:, 0:NE] = np.arange(NE)
    misc[:, 16:32] = np.tile(EG - np.arange(EG), NG)
    misc[:, 32:37] = np.arange(NT)[None, :] * P + np.arange(P)[:, None]
    return {"c_ident": ident, "c_masks": masks, "c_sel": sel, "c_eye4": eye4,
            "c_rope": np.ascontiguousarray(rope), "c_misc": misc}


def build(nc, a, out, scratch):
    with ExitStack() as ctx:
        build_body(nc, ctx, a, out, scratch)


def build_body(nc, ctx, a, out, scratch):
    def sb(name, shape, dt=F32):
        return ctx.enter_context(nc.sbuf_tensor(name, shape, dt))

    def sem(name):
        return ctx.enter_context(nc.semaphore(name))

    hT = sb("hT", [P, KD * T])
    PR = sb("PR", [P, 20500])
    HM = sb("HM", [P, NT * 512])
    RING = sb("RING", [P, 2 * KD * 512])
    TMP = sb("TMP", [P, 10520])
    PS = ctx.enter_context(nc.psum_tensor("PS", [P, 8, 512], F32))

    ident = sb("ident", [P, P])
    identb = sb("identb", [P, P], BF16)
    masks = sb("masks", [P, 4, P])
    masksb = sb("masksb", [P, 4, P], BF16)
    sel = sb("sel", [H, H, P])
    ones4 = sb("ones4", [H, P])
    eye4 = sb("eye4", [H, NT, H])
    rope = sb("rope", [P, 2, 4, QK])
    misc = sb("misc", [P, 64])
    fnorm = sb("fnorm", [P, D])
    wgate = sb("wgate", [P, KD, 16])
    wroute = sb("wroute", [P, KD, 20])
    vrows = sb("vrows", [40, P])
    cols = sb("cols", [P, 40])
    silc = sb("silc", [P, KD, 2])
    modc = sb("modc", [P, 16, 2])
    lamb = sb("lamb", [P, 4, QK])
    lam = sb("lam", [P, 8])
    bgate = sb("bgate", [P, 16])
    broute = sb("broute", [P, 20])
    stat = sb("stat", [P, 64])
    gtok = sb("gtok", [P, NT, 16])
    sm_in = sb("sm_in", [H, 2])
    m0b = sb("m0b", [P, 2, H])
    mendd = sb("mendd", [H, 2, NT, H])
    mend = sb("mend", [P, 2, NT, H])
    mprev = sb("mprev", [P, 2, NT, H])
    gcol = sb("gcol", [P, 3, 2, NT, H])
    coef = sb("coef", [P, 4, 2, NT, H])
    nout = sb("nout", [P, 2, H])
    newm = sb("newm", [H, 2])

    x_in = PR[:, 15380:20500].rearrange("p (t d) -> p t d", t=NT)
    xn = PR[:, 10260:12308].rearrange("p (b d) -> p b d", b=2)
    junk = PR[:, 12820:13844]
    hTv = hT[:, :].rearrange("p (k t) -> p k t", k=KD)
    mk_tok = PR[:, 0:2560].rearrange("p (t h d) -> p t h d", t=NT, h=H)
    mv1 = PR[:, 2560:5140].rearrange("p (t h d) -> p t h d", t=NT, h=H)
    sgo = PR[:, 5140:7700].rearrange("p (t d) -> p t d", t=NT)
    dv_tok = PR[:, 7700:10260].rearrange("p (t h d) -> p t h d", t=NT, h=H)
    mqT, mkT, dqT, dkT = (PR[:, 10260 + 2560 * i:12820 + 2560 * i].rearrange("p (h t) -> p h t", h=H)
                          for i in range(4))
    hm = HM[:, :].rearrange("p (t h d) -> p t h d", t=NT, h=H)
    ada_b = HM[0:2, 0:1024].rearrange("p (b n) -> p b n", b=2)
    ada_g = HM[0:2, 1024:2048]
    ring = RING[:, :].rearrange("p (b k n) -> p b k n", b=2, k=KD)

    gi = TMP[0:H, 0:1280].rearrange("p (d t) -> p d t", d=2)
    ee = TMP[0:H, 1280:2560].rearrange("p (d t) -> p d t", d=2)
    gf = TMP[0:H, 9240:10520].rearrange("p (d t) -> p d t", d=2)
    xr = TMP[:, 2560:3584].rearrange("p (b n) -> p b n", b=2)
    xs = TMP[:, 3584:4608].rearrange("p (b n) -> p b n", b=2)
    rr = TMP[:, 4608:5632].rearrange("p (b n) -> p b n", b=2)
    grow = TMP[0:16, 3584:4224]
    gzero = TMP[0:H, 4608:5120]
    wexp = TMP[:, 0:1024].rearrange("p (b h t) -> p b h t", b=2, h=H)
    sw = TMP[:, 1024:2048].rearrange("p (b h t) -> p b h t", b=2, h=H)
    CT = TMP[:, 2048:4112].rearrange("p (d b h v) -> p d b h v", d=2, b=2, h=H)
    num = TMP[:, 4112:4628].rearrange("p (h v) -> p h v", h=H)
    kw = TMP[:, 4628:5652].rearrange("p (b h k) -> p b h k", b=2, h=H)
    newC = TMP[:, 5652:6676].rearrange("p (e k) -> p e k", e=8)
    sC = TMP[:, 6676:7700].rearrange("p (e k) -> p e k", e=8)
    kc = TMP[:, 7700:8212]
    vc = TMP[:, 8212:8724].rearrange("p (h d) -> p h d", h=H)
    ckT = TMP[:, 8724:9236].rearrange("p (h t) -> p h t", h=H)
    pexp = TMP[:, 0:2560].rearrange("p (b m k) -> p b m k", b=2, m=2)
    aT = TMP[:, 2560:3840].rearrange("p (b t q) -> p b t q", b=2, t=5)
    hd = TMP[:, 3840:4864].rearrange("p (b h d) -> p b h d", b=2, h=H)
    x1 = TMP[:, 0:5120].rearrange("p (t d) -> p t d", t=NT)
    mod2 = TMP[:, 5120:9216].rearrange("p (s c d) -> p s c d", s=2, c=2)
    g1b = HM[:, 0:2048].rearrange("p (c d) -> p c d", c=2)
    g2b = PR[:, 18432:20480].rearrange("p (c d) -> p c d", c=2)
    h2 = PR[:, 12288:14336].rearrange("p (b d) -> p b d", b=2)
    junkn = PR[:, 14336:15360]
    mixg = PR[:, 15380:16404].rearrange("p (b n) -> p b n", b=2)
    hsq = PR[:, 10260:12820].rearrange("p (g d) -> p g d", d=HD)
    hdq = TMP[:, 4864:5376].rearrange("p (h d) -> p h d", h=H)
    gub = [PR[:, 6144 * b:6144 * b + 4096].rearrange("p (k n) -> p k n", k=KD) for b in range(2)]
    dnb = [PR[:, 6144 * b + 4096:6144 * b + 6144].rearrange("p (k n) -> p k n", k=2) for b in range(2)]
    xg = RING[:, 0:2048].rearrange("p (b d) -> p b d", b=2)
    xgT = RING[:, 2048:4096].rearrange("p (b k s) -> p b k s", b=2, k=KD)
    hid = RING[:, 4096:4608].rearrange("p (b n) -> p b n", b=2)
    hidT = RING[:, 4608:5120].rearrange("p (b k s) -> p b k s", b=2, k=2)
    sil = RING[:, 5120:5632].rearrange("p (b n) -> p b n", b=2)
    yo = RING[:, 5632:7680].rearrange("p (b d) -> p b d", b=2)
    ypick = hT[:, 0:4096].rearrange("p (b j d) -> p b j d", b=2, j=2)

    lgt = sb("lgt", [P, NT, 20])
    rt = sb("rt", [P, 12, NT, 4])
    rs = sb("rs", [P, 24, NT])
    r16 = sb("r16", [P, 3, NT, NE])
    ohb = sb("ohb", [P, NT, NE], BF16)
    slot = sb("slot", [P, 4, NT], U32)
    tokid = sb("tokid", [P, NT], U32)
    idall = sb("idall", [P, NE], U32)
    idp = sb("idp", [P, 2], U32)
    cnt = sb("cnt", [P, 4])
    rnd = sb("rnd", [P, 1], I32)
    zid = sb("zid", [P, ROUNDS * NE], U32)

    x_loaded = [sem(f"x_loaded{t}") for t in range(NT)]
    vec_loaded = sem("vec_loaded")
    small_loaded = sem("small_loaded")
    cache_loaded = sem("cache_loaded")
    state_loaded = sem("state_loaded")
    bias_loaded = [sem(f"bias_loaded{b}") for b in range(2)]
    row_stored = sem("row_stored")
    half_in = [sem(f"half_in{i}") for i in range(4)]
    chunk_used = sem("chunk_used")
    consts_ready = sem("consts_ready")
    cols_T = sem("cols_T")
    cols_ready = sem("cols_ready")
    silc_ready = sem("silc_ready")
    sumsq = sem("sumsq")
    rstd_ready = sem("rstd_ready")
    xn_ready = sem("xn_ready")
    xnT_done = sem("xnT_done")
    hraw_a = sem("hraw_a")
    hraw_v = sem("hraw_v")
    ada_done = sem("ada_done")
    ada_row = sem("ada_row")
    adacol_T = sem("adacol_T")
    h_ready = sem("h_ready")
    gate_done = sem("gate_done")
    gate_tok = sem("gate_tok")
    gate_T = sem("gate_T")
    gate_rows = sem("gate_rows")
    gate_split = sem("gate_split")
    nabs_f = sem("nabs_f")
    softp = sem("softp")
    scans_done = sem("scans_done")
    gcol_T = sem("gcol_T")
    gcol_ready = sem("gcol_ready")
    mendd_ready = sem("mendd_ready")
    mend_bc = sem("mend_bc")
    coef_args = sem("coef_args")
    coef_ready = sem("coef_ready")
    mm_done = sem("mm_done")
    mm_evac = sem("mm_evac")
    win_T = sem("win_T")
    win_Tevac = sem("win_Tevac")
    roped = sem("roped")
    state_T = sem("state_T")
    ct0_ready = sem("ct0_ready")
    kw_ready = sem("kw_ready")
    mb_done = sem("mb_done")
    w_ready = sem("w_ready")
    st_done = sem("st_done")
    sw_ready = sem("sw_ready")
    upd_done = sem("upd_done")
    ct_ready = sem("ct_ready")
    num_done = sem("num_done")
    num_read = sem("num_read")
    hm_ready = sem("hm_ready")
    newC_T = sem("newC_T")
    newC_ready = sem("newC_ready")
    newn_ready = sem("newn_ready")
    outs = sem("outs")
    hn_sq = sem("hn_sq")
    hn_ss = sem("hn_ss")
    hn_rstd = sem("hn_rstd")
    hm_normed = sem("hm_normed")
    mix_T = sem("mix_T")
    mix_ready = sem("mix_ready")
    ck_T = sem("ck_T")
    ck_ready = sem("ck_ready")
    sc_done = sem("sc_done")
    smax = sem("smax")
    pexp_done = sem("pexp_done")
    a_ready = sem("a_ready")
    a_T = sem("a_T")
    aT_ready = sem("aT_ready")
    pv_done = sem("pv_done")
    pv_read = sem("pv_read")
    lam_args = sem("lam_args")
    lam_exp = sem("lam_exp")
    dstep = sem("dstep")
    astep = sem("astep")
    pstep = sem("pstep")
    xr_loaded = sem("xr_loaded")
    mod_loaded = sem("mod_loaded")
    g1_loaded = sem("g1_loaded")
    o_done = sem("o_done")
    o_evac = sem("o_evac")
    x1_ready = sem("x1_ready")
    n2_rstd = sem("n2_rstd")
    h2_ready = sem("h2_ready")
    h2_stored = [sem(f"h2_stored{b}") for b in range(2)]
    h2_T = sem("h2_T")
    h2T_ready = sem("h2T_ready")
    route_done = sem("route_done")
    route_exp = sem("route_exp")
    route_arg = sem("route_arg")
    oh_ready = sem("oh_ready")
    rank_done = sem("rank_done")
    slots_ready = sem("slots_ready")
    rounds_ready = sem("rounds_ready")
    zid_stored = sem("zid_stored")
    ids_stored = sem("ids_stored")
    idall_in = sem("idall_in")
    idp_ready = sem("idp_ready")
    wg_in = [sem(f"wg_in{b}") for b in range(2)]
    wd_in = [sem(f"wd_in{b}") for b in range(2)]
    wg_used = [sem(f"wg_used{b}") for b in range(2)]
    wd_used = [sem(f"wd_used{b}") for b in range(2)]
    xg_in = [sem(f"xg_in{b}") for b in range(2)]
    xg_T = [sem(f"xg_T{b}") for b in range(2)]
    xgT_ready = [sem(f"xgT_ready{b}") for b in range(2)]
    gu_done = [sem(f"gu_done{b}") for b in range(2)]
    sil_ready = [sem(f"sil_ready{b}") for b in range(2)]
    hid_ready = [sem(f"hid_ready{b}") for b in range(2)]
    hid_T = [sem(f"hid_T{b}") for b in range(2)]
    hidT_ready = [sem(f"hidT_ready{b}") for b in range(2)]
    dn_done = [sem(f"dn_done{b}") for b in range(2)]
    yo_ready = [sem(f"yo_ready{b}") for b in range(2)]
    yo_stored = [sem(f"yo_stored{b}") for b in range(2)]
    pool_turn = sem("pool_turn")
    pick_in = [sem(f"pick_in{b}") for b in range(2)]
    y_sum = sem("y_sum")
    x2_ready = sem("x2_ready")
    fin_rstd = sem("fin_rstd")
    fin_ready = sem("fin_ready")

    block = ctx.enter_context(nc.Block())

    MG = [(0, 0), (1, 0), (0, 1), (1, 4), (0, 2), (1, 3), (0, 3), (1, 2), (0, 4), (1, 1)]
    NMG = len(MG)
    NUPD = NMG - 2
    UNITS = [(t, h) for t in range(NT) for h in range(H)]
    NU = len(UNITS)
    PAIRS = NE // 2
    ADA2_N = list(range(4, 12))

    def keys(t):
        return P if t == 0 else LAT + PAST

    w_dram = {"ada": a["w_ada"][0], "out": a["w_out"][0]}

    @block.sync
    def _(sp):
        for t in range(NT):
            src = a["x_prompt"][0] if t == 0 else a["x_sample"][0, (t - 1) * P:t * P, :]
            sp.dma_start(x_in[:, t, :], src).then_inc(x_loaded[t], 16)
        for ci, (kind, col) in enumerate(CHUNKS):
            w = w_dram.get(kind, a["w_in"][0]).rearrange("(h k p) n -> h p k n", h=2, p=P)
            if ci >= 2:
                sp.wait_ge(chunk_used, ci - 1)
            for hf in range(2):
                sp.dma_start(ring[:, ci % 2, 4 * hf:4 * hf + 4, :],
                             w[hf, :, :, col:col + 512]).then_inc(half_in[2 * (ci % 2) + hf], 16)
        sp.wait_ge(mix_ready, 2 * NT)
        for t in range(NT):
            src = a["x_prompt"][0] if t == 0 else a["x_sample"][0, (t - 1) * P:t * P, :]
            sp.dma_start(x1[:, t, :], src).then_inc(xr_loaded, 16)
        sp.wait_ge(outs, 16 * 5)
        sp.wait_ge(row_stored, 16 * 8)
        rows = scratch["mod"]
        for c in range(2):
            sp.dma_start(g1b[:, c, :], rows[c, 0:D].partition_broadcast(P)).then_inc(g1_loaded, 16)
        for s in range(2):
            for c in range(2):
                sp.dma_start(mod2[:, s, c, :],
                             rows[c, D * (1 + s):D * (2 + s)].partition_broadcast(P)).then_inc(mod_loaded, 16)
        for c in range(2):
            sp.dma_start(g2b[:, c, :], rows[c, 3 * D:4 * D].partition_broadcast(P)).then_inc(mod_loaded, 16)
        w_gu = a["w_gate_up"][0].rearrange("e (k p) n -> p e k n", p=P)
        w_dn = a["w_down"][0].rearrange("e (k p) n -> p e k n", p=P)
        for b in range(2):
            sp.dma_start(gub[b], w_gu[:, b]).then_inc(wg_in[b], 16)
            sp.dma_start(dnb[b], w_dn[:, b]).then_inc(wd_in[b], 16)
        sp.wait_ge(rounds_ready, 1)
        n_rounds = sp.value_load(rnd[0:1, 0:1], min_val=1, max_val=ROUNDS)
        with sp.Fori(1, n_rounds * PAIRS) as it:
            first = (it % PAIRS) * 2
            for b in range(2):
                sp.wait_ge(wg_used[b], it)
                sp.dma_start(gub[b], w_gu[:, bass.ds(first + b, 1)].rearrange("p e k n -> p (e k) n")
                             ).then_inc(wg_in[b], 16)
                sp.wait_ge(wd_used[b], it)
                sp.dma_start(dnb[b], w_dn[:, bass.ds(first + b, 1)].rearrange("p e k n -> p (e k) n")
                             ).then_inc(wd_in[b], 16)
        for t in range(NT):
            sp.wait_ge(fin_ready, t + 1)
            dst = out["y_prompt"][0] if t == 0 else out["y_sample"][0, (t - 1) * P:t * P, :]
            sp.dma_start(dst, x1[:, t, :]).then_inc(outs, 16)
        sp.wait_ge(outs, 16 * (NT + 5))

    @block.gpsimd
    def _(pool):
        n = [0]

        def step(ins):
            n[0] += 1
            ins.then_inc(pstep, 1)
            pool.wait_ge(pstep, n[0])

        pool.dma_start(vrows[0:8, :], a["c_ctx"].rearrange("(k p) -> k p", p=P)).then_inc(vec_loaded, 16)
        pool.dma_start(vrows[8:16, :], a["c"][0].rearrange("(k p) -> k p", p=P)).then_inc(vec_loaded, 16)
        pool.dma_start(vrows[16:24, :], a["norm_mix"][0].rearrange("(k p) -> k p", p=P)).then_inc(vec_loaded, 16)
        pool.dma_start(vrows[24:28, :], a["mlstm_norm"][0].rearrange("(k p) -> k p", p=P)).then_inc(vec_loaded, 16)
        pool.dma_start(vrows[28:32, :], a["diff_norm"][0].rearrange("(k p) -> k p", p=P)).then_inc(vec_loaded, 16)
        pool.dma_start(vrows[32:40, :], a["state_n"][0, 0].rearrange("d h k -> (d h) k")).then_inc(vec_loaded, 16)
        pool.dma_start(ident[:], a["c_ident"]).then_inc(vec_loaded, 16)
        small = [(masks[:], a["c_masks"]), (sel[:], a["c_sel"]), (eye4[:], a["c_eye4"]),
                 (rope[:], a["c_rope"]), (misc[:], a["c_misc"]),
                 (wgate[:], a["w_in"][0].rearrange("(k p) n -> p k n", p=P)[:, :, OFF["gate"]:OFF["gate"] + 16]),
                 (wroute[:, :, 0:4], a["w_route_group"][0].rearrange("(k p) n -> p k n", p=P)),
                 (wroute[:, :, 4:20], a["w_route_expert"][0].rearrange("(k p) n -> p k n", p=P)),
                 (bgate[:], a["b_gate"][0].partition_broadcast(P)),
                 (broute[:, 0:4], a["b_route_group"][0].partition_broadcast(P)),
                 (broute[:, 4:20], a["b_route_expert"][0].partition_broadcast(P)),
                 (lamb[:], a["diff_lambda"][0].partition_broadcast(P)),
                 (fnorm[:], a["final_norm"].partition_broadcast(P)),
                 (sm_in[:], a["state_m"][0, 0].rearrange("d h -> h d")),
                 (m0b[:], a["state_m"][0, 0].partition_broadcast(P)),
                 (ada_g, a["norm_ffn"][0].partition_broadcast(2))]
        assert len(small) == SMALL
        for dst, src in small:
            pool.dma_start(dst, src, allow_slow_non_contiguous=dst.shape == (H, 2)).then_inc(small_loaded, 16)
        bias = a["b_ada"][0]
        for c in range(2):
            pool.dma_start(ada_b[:, c, :], bias[c * 512:(c + 1) * 512].partition_broadcast(2)).then_inc(bias_loaded[c], 16)
        nc.gpsimd.memset(zid[:], 0).then_inc(consts_ready, 1)
        nc.gpsimd.memset(ones4[:], 1.0).then_inc(consts_ready, 1)
        nc.gpsimd.memset(stat[:, 60:61], EPS).then_inc(consts_ready, 1)
        pool.wait_ge(consts_ready, 3)
        pool.dma_start(scratch["ids"].rearrange("(p n) o -> p (n o)", p=P), zid[:]).then_inc(zid_stored, 16)
        for n_ in range(2, 12):
            if n_ - 2 < 4:
                pool.wait_ge(adacol_T, n_ - 1)
            else:
                pool.wait_ge(ada_row, n_ - 1)
                pool.dma_start(scratch["mod"][:, (n_ - 6) * 512:(n_ - 5) * 512], ada_b[:, n_ % 2, :]).then_inc(row_stored, 16)
                pool.wait_ge(row_stored, 16 * (n_ - 5))
            pool.dma_start(ada_b[:, n_ % 2, :], bias[n_ * 512:(n_ + 1) * 512].partition_broadcast(2)
                           ).then_inc(bias_loaded[n_ % 2], 16)
            if n_ == 4:
                pool.wait_ge(gate_rows, 1)
                for g, dst in enumerate((gi[:, 0, :], gf[:, 0, :], gi[:, 1, :], gf[:, 1, :])):
                    pool.dma_start(dst, grow[4 * g:4 * g + 4, :]).then_inc(gate_split, 16)
                pool.dma_start(kc, a["cache_k"][0, 0].rearrange("t h m d -> t (h m d)")).then_inc(cache_loaded, 16)
                pool.dma_start(vc, a["cache_v"][0, 0]).then_inc(cache_loaded, 16)
                pool.dma_start(sC, a["state_C"][0, 0].rearrange("d h v k -> v (d h) k")).then_inc(state_loaded, 16)
        for n_ in range(10, 12):
            pool.wait_ge(ada_row, n_ + 1)
            pool.dma_start(scratch["mod"][:, (n_ - 4) * 512:(n_ - 3) * 512], ada_b[:, n_ % 2, :]).then_inc(row_stored, 16)
        pool.wait_ge(row_stored, 16 * 8)
        pool.wait_ge(coef_ready, 1)
        pool.wait_ge(mm_evac, NT)
        for g, (d, t) in enumerate(MG[:NUPD]):
            if g >= 2:
                pool.wait_ge(upd_done, g - 1)
            nc.gpsimd.tensor_tensor(kw[:, g % 2], mk_tok[:, t], coef[:, 0, d, t, :].unsqueeze(2).broadcast_to([P, H, HD]),
                                    ALU.mult).then_inc(kw_ready, 1)
        pool.wait_ge(slots_ready, 1)
        pool.wait_ge(zid_stored, 16)
        for t in range(NT):
            for j in range(2):
                pool.indirect_dma_start(out=scratch["ids"], out_offset=bass.IndirectOffsetOnAxis(ap=slot[:, j, t:t + 1], axis=0),
                                        in_=tokid[:, t:t + 1], in_offset=None).then_inc(ids_stored, 16)
        pool.wait_ge(ids_stored, 16 * 2 * NT)
        pool.wait_ge(h2_stored[0], 16 * 3)
        pool.wait_ge(h2_stored[1], 16 * 2)
        pool.wait_ge(rounds_ready, 1)
        n_rounds = pool.value_load(rnd[0:1, 0:1], min_val=1, max_val=ROUNDS)
        with pool.Fori(0, n_rounds) as r:
            pool.dma_start(idall[:], scratch["ids"][bass.ds(r * (P * NE), P * NE), :].rearrange("(p e) o -> p (e o)", e=NE)
                           ).then_inc(idall_in, 16)
            pool.wait_ge(idall_in, 16 * (r + 1))
            pool.sem_inc(pool_turn, 1)
            with pool.Fori(0, PAIRS) as q:
                it = r * PAIRS + q
                for b in range(2):
                    pool.wait_ge(xg_T[b], it + 1)
                nc.gpsimd.tensor_copy(idp[:], idall[:, bass.ds(q * 2, 2)]).then_inc(idp_ready, 1)
                pool.wait_ge(idp_ready, it + 1)
                pool.sem_inc(pool_turn, 1)
                for b in range(2):
                    pool.indirect_dma_start(out=xg[:, b, :], out_offset=None, in_=scratch["h2"],
                                            in_offset=bass.IndirectOffsetOnAxis(ap=idp[:, b:b + 1], axis=0)
                                            ).then_inc(xg_in[b], 16)
            for b in range(2):
                pool.wait_ge(yo_stored[b], r * (PAIRS * 16) + (PAIRS * 16 + 16))
            for t in range(NT):
                pool.wait_ge(y_sum, r * NT + (2 if t == 0 else t if t == 1 else t + 1))
                pool.sem_inc(pool_turn, 1)
                for j in range(2):
                    pool.indirect_dma_start(out=ypick[:, t % 2, j, :], out_offset=None, in_=scratch["y"],
                                            in_offset=bass.IndirectOffsetOnAxis(ap=slot[:, 2 + j, t:t + 1], axis=0)
                                            ).then_inc(pick_in[t % 2], 16)
            for b in range(2):
                pool.wait_ge(pick_in[b], r * (32 * (3 - b)) + 32 * (3 - b))
            pool.sem_inc(pool_turn, 1)

    @block.scalar
    def _(act):
        n = [0]

        def step(ins):
            n[0] += 1
            ins.then_inc(astep, 1)
            act.wait_ge(astep, n[0])

        for t in range(NT):
            act.wait_ge(x_loaded[t], 16)
            step(nc.scalar.activation(junk, x_in[:, t, :], ACT.Square, accum_out=stat[:, t:t + 1]))
        act.wait_ge(consts_ready, 3)
        step(nc.scalar.activation(stat[:, 8:8 + NT], stat[:, 0:NT], ACT.Ln, scale=1.0 / D, bias=stat[:, 60:61]))
        nc.scalar.activation(stat[:, 16:16 + NT], stat[:, 8:8 + NT], ACT.Exp, scale=-0.5).then_inc(rstd_ready, 1)
        act.wait_ge(cols_ready, 1)
        nc.scalar.activation(silc[:].rearrange("p k c -> p c k"), cols[:, 0:16].rearrange("p (c k) -> p c k", c=2),
                             ACT.Silu).then_inc(silc_ready, 1)
        for t in range(NT):
            act.wait_ge(xnT_done, t + 1)
            nc.scalar.activation(hTv[:, 0:4, t * P:(t + 1) * P],
                                 PS[:, 2 * (t % 2), :].rearrange("p (k s) -> p k s", k=4), ACT.Copy).then_inc(hraw_a, 1)
        rc = 0
        for c, w in enumerate(WIN_ORDER):
            for t in range(NT):
                m = c * NT + t
                act.wait_ge(mm_done, m + 1)
                src = PS[:, m % 4, :]
                qs = float(QK) ** -0.5 if w == "dq" else 1.0
                if w == "mk":
                    nc.scalar.activation(mk_tok[:, t], src.rearrange("p (h d) -> p h d", h=H), ACT.Copy,
                                         scale=float(HD) ** -0.5).then_inc(mm_evac, 1)
                elif w == "mv":
                    nc.scalar.activation(mv1[:, t, :, 0:HD], src.rearrange("p (h d) -> p h d", h=H),
                                         ACT.Copy).then_inc(mm_evac, 1)
                elif w == "mo":
                    nc.scalar.activation(sgo[:, t], src, ACT.Sigmoid).then_inc(mm_evac, 1)
                elif w == "dv":
                    nc.scalar.activation(dv_tok[:, t], src.rearrange("p (h d) -> p h d", h=H),
                                         ACT.Copy).then_inc(mm_evac, 1)
                else:
                    if rc >= 2:
                        act.wait_ge(win_T, NT + rc - 1)
                    if w != "mq" and t > 0:
                        if w == "dk" and t == 1:
                            act.wait_ge(gate_split, 64)
                        dst = xs[:, rc % 2].rearrange("p (g h j) -> p g h j", h=2, j=16)
                        s4 = src.rearrange("p (g h j) -> p g h j", h=2, j=16)
                        nc.scalar.activation(dst[:, :, 0, :], s4[:, :, 1, :], ACT.Copy, scale=qs)
                        nc.scalar.activation(dst[:, :, 1, :], s4[:, :, 0, :], ACT.Copy, scale=qs)
                    nc.scalar.activation(xr[:, rc % 2], src, ACT.Copy, scale=qs).then_inc(mm_evac, 1)
                    if w == "dk" and t == 0:
                        act.wait_ge(mm_evac, m + 1)
                        act.dma_start(out["new_k"][0, 0].rearrange("t h m d -> t (h m d)"), xr[:, rc % 2]).then_inc(outs, 16)
                        act.wait_ge(outs, 16)
                    rc += 1
                if w == "dv" and t == 0:
                    act.wait_ge(mm_evac, m + 1)
                    act.dma_start(out["new_v"][0, 0].rearrange("t h d -> t (h d)"),
                                  PR[:, 7700:8212]).then_inc(outs, 16)
                if w == "mq" and t == 0:
                    act.wait_ge(nabs_f, 1)
                    step(nc.scalar.activation(ee, ee, ACT.Exp))
                    nc.scalar.activation(ee, ee, ACT.Ln, bias=1.0).then_inc(softp, 1)
                if w == "mv" and t == 0:
                    act.wait_ge(coef_args, 1)
                    nc.scalar.activation(coef[:], coef[:], ACT.Exp).then_inc(coef_ready, 1)
        act.wait_ge(lam_args, 1)
        nc.scalar.activation(lam[:, 2:4], lam[:, 0:2], ACT.Exp).then_inc(lam_exp, 1)
        for g, (d, t) in enumerate(MG):
            act.wait_ge(mb_done, g + 1)
            if g >= 2:
                act.wait_ge(sw_ready, g - 1)
            for h in range(H):
                ins = nc.scalar.activation(wexp[:, g % 2, h, :], PS[:, 1, h * P:(h + 1) * P], ACT.Exp,
                                           bias=gcol[:, 0, d, t, h:h + 1], scale=-1.0)
            ins.then_inc(w_ready, 1)
            if g < 2:
                act.wait_ge(newC_T, g + 1)
                nc.scalar.activation(newC[:, 4 * d:4 * d + 4, :], PS[:, 6 + d, :].rearrange("p (h k) -> p h k", h=H),
                                     ACT.Copy).then_inc(newC_ready, 1)
        act.wait_ge(newC_ready, 2)
        act.dma_start(out["new_C"][0, 0].rearrange("d h v k -> v (d h) k"), newC).then_inc(outs, 16)
        act.wait_ge(ct_ready, 2)
        act.dma_start(out["new_n"][0, 0].rearrange("d h k -> k d h"), nout[:], allow_slow_non_contiguous=True).then_inc(outs, 16)
        act.dma_start(out["new_m"][0, 0].rearrange("d h -> h d"), newm[:], allow_slow_non_contiguous=True).then_inc(outs, 16)
        act.wait_ge(hn_ss, 1)
        step(nc.scalar.activation(stat[:, 20:40], stat[:, 20:40], ACT.Ln, scale=1.0 / HD, bias=stat[:, 60:61]))
        nc.scalar.activation(stat[:, 20:40], stat[:, 20:40], ACT.Exp, scale=-0.5).then_inc(hn_rstd, 1)
        for t in range(NT):
            act.wait_ge(mix_T, t + 1)
            for h in range(H):
                ins = nc.scalar.activation(hTv[:, h, t * P:(t + 1) * P], PS[:, 6 + t % 2, h * P:(h + 1) * P], ACT.Copy,
                                           scale=cols[:, 24 + h:25 + h])
            ins.then_inc(mix_ready, 1)
        for u in range(NU + 2):
            if u < NU:
                nk = keys(UNITS[u][0])
                for m in range(2):
                    act.wait_ge(smax, 2 * u + m + 1)
                    if u >= 2 and m == 0:
                        act.wait_ge(a_T, u - 1)
                    nc.scalar.activation(pexp[:, u % 2, m, 0:nk],
                                         PS[:, 2 * m:2 * m + 2, :].rearrange("p b n -> p (b n)")[:, 0:nk], ACT.Exp,
                                         bias=stat[:, 40 + m:41 + m],
                                         accum_out=stat[:, 42 + 2 * (u % 2) + m:43 + 2 * (u % 2) + m]
                                         ).then_inc(pexp_done, 1)
            if 1 <= u <= NU:
                nk = keys(UNITS[u - 1][0])
                act.wait_ge(a_T, u)
                if u >= 3:
                    act.wait_ge(pv_done, u - 2)
                nc.scalar.activation(aT[:, (u - 1) % 2].rearrange("p t q -> p (t q)")[:, 0:nk],
                                     PS[:, 4:6, :].rearrange("p b n -> p (b n)")[:, 0:nk], ACT.Copy).then_inc(aT_ready, 1)
                t, h = UNITS[u - 1]
                if h == H - 1:
                    act.wait_ge(hn_ss, 2 + t)
                    step(nc.scalar.activation(stat[:, 52:56], stat[:, 48:52], ACT.Ln, scale=1.0 / HD, bias=stat[:, 60:61]))
                    nc.scalar.activation(stat[:, 52:56], stat[:, 52:56], ACT.Exp, scale=-0.5).then_inc(hn_rstd, 1)
            if u >= 2 and UNITS[u - 2][1] == H - 1:
                t = UNITS[u - 2][0]
                act.wait_ge(mix_T, NT + t + 1)
                for hh in range(H):
                    ins = nc.scalar.activation(hTv[:, 4 + hh, t * P:(t + 1) * P], PS[:, 7, hh * P:(hh + 1) * P],
                                               ACT.Copy, scale=cols[:, 28 + hh:29 + hh])
                ins.then_inc(mix_ready, 1)
        for t in range(NT):
            act.wait_ge(x1_ready, 2 * (t + 1))
            step(nc.scalar.activation(junkn, x1[:, t, :], ACT.Square, accum_out=stat[:, t:t + 1]))
            step(nc.scalar.activation(stat[:, 8 + t:9 + t], stat[:, t:t + 1], ACT.Ln, scale=1.0 / D, bias=stat[:, 60:61]))
            nc.scalar.activation(stat[:, 16 + t:17 + t], stat[:, 8 + t:9 + t], ACT.Exp, scale=-0.5).then_inc(n2_rstd, 1)
            act.wait_ge(h2_ready, t + 1)
            act.dma_start(scratch["h2"][t * P:(t + 1) * P, :], h2[:, t % 2, :]).then_inc(h2_stored[t % 2], 16)
            act.wait_ge(h2_T, t + 1)
            for k2 in range(2):
                ins = nc.scalar.activation(hTv[:, 4 * k2:4 * k2 + 4, t * P:(t + 1) * P],
                                           PS[:, 4 + k2, :].rearrange("p (k s) -> p k s", k=4), ACT.Copy)
            ins.then_inc(h2T_ready, 1)
        act.wait_ge(route_arg, 1)
        nc.scalar.activation(rt[:, 1], rt[:, 1], ACT.Exp).then_inc(route_exp, 1)
        nc.scalar.activation(rs[:, 2, :], rs[:, 2, :], ACT.Exp).then_inc(route_exp, 1)
        act.wait_ge(rounds_ready, 1)
        n_rounds = act.value_load(rnd[0:1, 0:1], min_val=1, max_val=ROUNDS)
        for b in range(2):
            act.sem_inc(yo_ready[b], 1)
            act.sem_inc(yo_stored[b], 16)
        with act.Fori(0, n_rounds * PAIRS) as it:
            for b in range(2):
                act.wait_ge(xg_T[b], it + 2)
                act.wait_ge(gu_done[b], it + 1)
                for k2 in range(2):
                    ins = nc.scalar.activation(xgT[:, b, 4 * k2:4 * k2 + 4, :],
                                               PS[:, 2 * b + k2, :].rearrange("p (k s) -> p k s", k=4), ACT.Copy)
                ins.then_inc(xgT_ready[b], 1)
            for b in range(2):
                act.wait_ge(gu_done[b], it + 2)
                nc.scalar.activation(sil[:, b, :], PS[:, 4 + b, 0:EH], ACT.Silu).then_inc(sil_ready[b], 1)
            for b in range(2):
                act.wait_ge(dn_done[b], it + 2)
                act.wait_ge(yo_stored[b], 16 * it + 16)
                nc.scalar.activation(yo[:, b, 0:512], PS[:, 2 * b, :], ACT.Copy)
                nc.scalar.activation(yo[:, b, 512:D], PS[:, 2 * b + 1, :], ACT.Copy).then_inc(yo_ready[b], 1)
                act.wait_ge(yo_ready[b], it + 2)
                act.dma_start(scratch["y"][bass.ds((it % PAIRS) * 256 + b * P, P), :], yo[:, b, :]).then_inc(yo_stored[b], 16)
        for t in range(NT):
            act.wait_ge(x2_ready, 1)
            step(nc.scalar.activation(junkn, x1[:, t, :], ACT.Square, accum_out=stat[:, t:t + 1]))
            step(nc.scalar.activation(stat[:, 8 + t:9 + t], stat[:, t:t + 1], ACT.Ln, scale=1.0 / D, bias=stat[:, 60:61]))
            nc.scalar.activation(stat[:, 16 + t:17 + t], stat[:, 8 + t:9 + t], ACT.Exp, scale=-0.5).then_inc(fin_rstd, 1)

    @block.vector
    def _(dve):
        n = [0]
        V = nc.vector

        def step(ins):
            n[0] += 1
            ins.then_inc(dstep, 1)
            dve.wait_ge(dstep, n[0])

        dve.wait_ge(cols_T, 1)
        V.tensor_copy(cols[:, 0:28], PS[:, 7, 0:28])
        V.tensor_scalar(cols[:, 28:32], PS[:, 7, 28:32], 1.0 - LAM_INIT, None, ALU.mult)
        V.tensor_copy(cols[:, 32:40], PS[:, 7, 32:40]).then_inc(cols_ready, 1)
        dve.wait_ge(rstd_ready, 1)
        for t in range(NT):
            if t >= 2:
                dve.wait_ge(xnT_done, t - 1)
            V.tensor_scalar(xn[:, t % 2, :], x_in[:, t, :], stat[:, 16 + t:17 + t], None, ALU.mult).then_inc(xn_ready, 1)
            if t >= 1:
                dve.wait_ge(xnT_done, t)
                V.tensor_copy(hTv[:, 4:8, (t - 1) * P:t * P],
                              PS[:, 2 * ((t - 1) % 2) + 1, :].rearrange("p (k s) -> p k s", k=4)).then_inc(hraw_v, 1)
        dve.wait_ge(xnT_done, NT)
        V.tensor_copy(hTv[:, 4:8, (NT - 1) * P:NT * P],
                      PS[:, 2 * ((NT - 1) % 2) + 1, :].rearrange("p (k s) -> p k s", k=4)).then_inc(hraw_v, 1)
        dve.wait_ge(small_loaded, 16 * SMALL)
        V.tensor_copy(identb[:], ident[:])
        V.tensor_copy(masksb[:], masks[:])
        V.tensor_copy(tokid[:], misc[:, 32:37])
        V.memset(gzero, 0.0)

        def ada_rows(n_):
            dve.wait_ge(ada_done, n_ + 1)
            dve.wait_ge(bias_loaded[n_ % 2], 16 * (n_ // 2 + 1))
            row = ada_b[:, n_ % 2, :]
            last = V.tensor_tensor(row, PS[0:2, 4 + n_ % 2, :], row, ALU.add)
            if n_ in (8, 9):
                step(last)
                last = V.scalar_tensor_tensor(row, row, 1.0, ada_g[:, (n_ - 8) * 512:(n_ - 7) * 512], ALU.add, ALU.mult)
            last.then_inc(ada_row, 1)

        for n_ in range(4):
            ada_rows(n_)
        dve.wait_ge(adacol_T, 4)
        V.tensor_copy(modc[:, 0:8, :], PS[:, 6, 0:16].rearrange("p (k c) -> p k c", c=2))
        step(V.scalar_tensor_tensor(modc[:, 8:16, :], PS[:, 6, 16:32].rearrange("p (k c) -> p k c", c=2), 1.0,
                                    cols[:, 16:24].unsqueeze(2).broadcast_to([P, KD, 2]), ALU.add, ALU.mult))
        dve.wait_ge(hraw_a, NT)
        dve.wait_ge(hraw_v, NT)
        for k in range(KD):
            for c, (lo, hi) in enumerate(((0, CTX), (CTX, T))):
                last = V.tensor_scalar(hTv[:, k, lo:hi], hTv[:, k, lo:hi], modc[:, 8 + k, c:c + 1], modc[:, k, c:c + 1],
                                       ALU.mult, ALU.add)
        last.then_inc(h_ready, 1)
        V.memset(mv1[:, :, :, HD:HD + 1], 1.0)
        dve.wait_ge(gate_done, 1)
        V.tensor_tensor(gtok[:], PS[:, 7, 0:80].rearrange("p (t g) -> p t g", t=NT),
                        bgate[:].unsqueeze(1).broadcast_to([P, NT, 16]), ALU.add).then_inc(gate_tok, 1)
        dve.wait_ge(gate_T, 1)
        V.tensor_copy(grow, PS[0:16, 6:8, :].rearrange("p b n -> p (b n)")[:, 0:T]).then_inc(gate_rows, 1)
        dve.wait_ge(gate_split, 64)
        step(V.scalar_tensor_tensor(ee, gf, -1.0, gf, ALU.mult, ALU.min))
        dve.sem_inc(nabs_f, 1)

        def win_evac(s, dst, t):
            dve.wait_ge(win_T, s + 1)
            V.tensor_copy(dst[:, :, t * P:(t + 1) * P], PS[:, 4 + s % 2, :].rearrange("p (h s) -> p h s", h=H)
                          ).then_inc(win_Tevac, 1)

        s = 0
        rc = 0
        for w, dst in (("mk", mkT), ("mq", mqT), ("dk", dkT), ("dq", dqT)):
            for t in range(NT):
                if w in ("dk", "dq") and t > 0:
                    m = WIN_ORDER.index(w) * NT + t
                    dve.wait_ge(mm_evac, m + 1)
                    if rc >= 2:
                        dve.wait_ge(win_T, s - 1)
                    b = rc % 2
                    g = lambda v: v.rearrange("p (g j) -> p g j", j=QK)
                    V.tensor_tensor(g(rr[:, b]), g(xr[:, b]), rope[:, 0, t - 1, :].unsqueeze(1).broadcast_to([P, 8, QK]), ALU.mult)
                    step(V.tensor_tensor(g(xs[:, b]), g(xs[:, b]), rope[:, 1, t - 1, :].unsqueeze(1).broadcast_to([P, 8, QK]), ALU.mult))
                    V.tensor_tensor(rr[:, b], rr[:, b], xs[:, b], ALU.add).then_inc(roped, 1)
                win_evac(s, dst, t)
                s += 1
                if w != "mk":
                    rc += 1
                if w == "mk" and t == NT - 1:
                    dve.wait_ge(softp, 1)
                    step(V.scalar_tensor_tensor(gf, gf, 0.0, ee, ALU.min, ALU.subtract))
                    spans = [(0, 0, CTX), (0, CTX, T), (1, 0, CTX), (1, CTX, T)]

                    def along(v, d, lo, hi):
                        return v[:, d, lo:hi] if d == 0 else v[:, d, lo:hi][:, ::-1]

                    for d, lo, hi in spans:
                        last = V.tensor_tensor_scan(along(ee, d, lo, hi), along(gf, d, lo, hi), gzero[:, 0:hi - lo],
                                                    0.0, ALU.add, ALU.add)
                    step(last)
                    step(V.tensor_tensor(gi, gi, ee, ALU.subtract))
                    for d, lo, hi in spans:
                        last = V.tensor_tensor_scan(along(gf, d, lo, hi), along(gi, d, lo, hi), gzero[:, 0:hi - lo],
                                                    0.0 if lo == 0 else sm_in[:, d:d + 1], ALU.max, ALU.add)
                    step(last)
                    step(V.tensor_tensor(ee, ee, gf, ALU.add))
                    V.tensor_copy(newm[:, 0:1], ee[:, 0, CTX - 1:CTX])
                    step(V.tensor_copy(newm[:, 1:2], ee[:, 1, 0:1]))
                    for d, e in ((0, P - 1), (1, 0)):
                        ends = gf[:, d, :].rearrange("p (t s) -> p t s", s=P)[:, :, e:e + 1].broadcast_to([H, NT, H])
                        last = V.tensor_tensor(mendd[:, d], ends, eye4[:], ALU.mult)
                    last.then_inc(mendd_ready, 1)
                    dve.wait_ge(gcol_T, 1)
                    V.tensor_copy(gcol[:].rearrange("p a d t h -> p (a d t h)"), PS[:, 6, 0:120]).then_inc(gcol_ready, 1)
                    dve.wait_ge(mend_bc, 1)
                    step(V.tensor_copy(mend[:].rearrange("p d t h -> p (d t h)"), PS[:, 7, 0:40]))
                    V.memset(mprev[:, :, 0, :], 0.0)
                    V.tensor_copy(mprev[:, 0, 2:5, :], mend[:, 0, 1:4, :])
                    V.tensor_copy(mprev[:, 1, 1:4, :], mend[:, 1, 2:5, :])
                    V.tensor_copy(mprev[:, 0, 1, :], m0b[:, 0, :])
                    step(V.tensor_copy(mprev[:, 1, 4, :], m0b[:, 1, :]))
                    V.tensor_tensor(coef[:, 0], gcol[:, 0], mend[:], ALU.subtract)
                    V.tensor_tensor(coef[:, 1], mprev[:], gcol[:, 1], ALU.subtract)
                    V.tensor_tensor(coef[:, 2], mprev[:], mend[:], ALU.subtract)
                    V.tensor_scalar(coef[:, 3], gcol[:, 2], -1.0, None, ALU.mult).then_inc(coef_args, 1)
        step(V.tensor_tensor(lamb[:, 0::2, :], lamb[:, 0::2, :], lamb[:, 1::2, :], ALU.mult))
        V.tensor_reduce(lam[:, 0:2], lamb[:, 0::2, :], AX.X, ALU.add).then_inc(lam_args, 1)
        for n_ in range(4, 12):
            ada_rows(n_)
        dve.wait_ge(lam_exp, 1)
        V.scalar_tensor_tensor(lam[:, 4:5], lam[:, 3:4], -LAM_INIT, lam[:, 2:3], ALU.add, ALU.subtract)
        dve.wait_ge(state_T, 1)
        for d in range(2):
            V.tensor_copy(CT[:, d, 0, :, 0:HD], PS[:, 6 + d, :].rearrange("p (h v) -> p h v", h=H))
            last = V.tensor_copy(CT[:, d, 0, :, HD:HD + 1], cols[:, 32 + 4 * d:36 + 4 * d].unsqueeze(2))
        last.then_inc(ct0_ready, 1)
        dve.wait_ge(ck_T, 1)
        V.tensor_copy(ckT, PS[:, 0, :].rearrange("p (h s) -> p h s", h=H)).then_inc(ck_ready, 1)

        two = lambda v: v.rearrange("p (b h) v -> p b h v", b=2)
        bank2 = lambda b: PS[:, b:b + 2, 0:258].rearrange("p b (h v) -> p b h v", h=2)
        seen = set()
        for g, (d, t) in enumerate(MG):
            dve.wait_ge(w_ready, g + 1)
            dve.wait_ge(st_done, g + 1)
            if g >= 2:
                dve.wait_ge(num_done, g - 1)
            V.tensor_tensor(sw[:, g % 2], PS[:, 0, :].rearrange("p (h t) -> p h t", h=H), wexp[:, g % 2],
                            ALU.mult).then_inc(sw_ready, 1)
            if g < NUPD:
                i = (g // 2) - 1
                dve.wait_ge(upd_done, g + 1)
                if i < 0:
                    V.tensor_copy(two(CT[:, d, 1]), bank2(6))
                    last = V.tensor_copy(nout[:, d, :], PS[:, 6:8, 0:258].rearrange("p b (h v) -> p b h v", h=2)[:, :, :, HD])
                    last.then_inc(ct_ready, 1)
                else:
                    dec = coef[:, 2, d, t, :].unsqueeze(2).broadcast_to([P, H, HD + 1])
                    src, dst = CT[:, d, i % 2], CT[:, d, (i + 1) % 2]
                    dve.wait_ge(num_done, g - 1)
                    step(V.tensor_tensor(dst, src, dec, ALU.mult))
                    V.tensor_tensor(two(dst), two(dst), bank2(6), ALU.add).then_inc(ct_ready, 1)
            dve.wait_ge(num_done, g + 1)
            if t == 0:
                step(V.tensor_copy(two(num), bank2(2)))
            else:
                ws = coef[:, 1, d, t, :].rearrange("p (b h) -> p b h", b=2).unsqueeze(3).broadcast_to([P, 2, 2, HD + 1])
                step(V.tensor_tensor(two(num), bank2(4), ws, ALU.mult))
                step(V.tensor_tensor(two(num), two(num), bank2(2), ALU.add))
            dve.sem_inc(num_read, 1)
            den = stat[:, 56:60]
            step(V.scalar_tensor_tensor(den, num[:, :, HD], -1.0, num[:, :, HD], ALU.mult, ALU.max))
            step(V.tensor_tensor(den, den, coef[:, 3, d, t, :], ALU.max))
            step(V.reciprocal(den, den))
            rb_ = den.unsqueeze(2).broadcast_to([P, H, HD])
            if t not in seen:
                seen.add(t)
                step(V.tensor_tensor(hm[:, t], num[:, :, 0:HD], rb_, ALU.mult))
            else:
                step(V.tensor_tensor(num[:, :, 0:HD], num[:, :, 0:HD], rb_, ALU.mult))
                step(V.tensor_tensor(hm[:, t], hm[:, t], num[:, :, 0:HD], ALU.add))
        hmf = HM[:, :].rearrange("p (g d) -> p g d", d=HD)
        step(V.tensor_tensor(hsq, hmf, hmf, ALU.mult))
        V.tensor_reduce(stat[:, 20:40], hsq, AX.X, ALU.add).then_inc(hn_ss, 1)
        dve.wait_ge(hn_rstd, 1)
        for t in range(NT):
            rb_ = stat[:, 20 + 4 * t:24 + 4 * t].unsqueeze(2).broadcast_to([P, H, HD])
            step(V.tensor_tensor(hm[:, t], hm[:, t], rb_, ALU.mult))
            V.tensor_tensor(hm[:, t], hm[:, t], sgo[:, t].rearrange("p (h d) -> p h d", h=H), ALU.mult).then_inc(hm_normed, 1)
        for u in range(NU + 2):
            if u < NU:
                t, h = UNITS[u]
                nk = keys(t)
                for m in range(2):
                    dve.wait_ge(sc_done, 2 * u + m + 1)
                    if u >= 1:
                        dve.wait_ge(pexp_done, 2 * (u - 1) + m + 1)
                    V.tensor_reduce(stat[:, 40 + m:41 + m], PS[:, 2 * m:2 * m + 2, :].rearrange("p b n -> p (b n)")[:, 0:nk],
                                    AX.X, ALU.max, negate=True).then_inc(smax, 1)
            if 1 <= u <= NU:
                t, h = UNITS[u - 1]
                dve.wait_ge(pv_done, u)
                last = V.tensor_scalar(hd[:, t % 2, h, :], PS[:, 6, h * HD:(h + 1) * HD],
                                       stat[:, 46 + (u - 1) % 2:47 + (u - 1) % 2], None, ALU.mult)
                last.then_inc(pv_read, 1)
                if h == H - 1:
                    dve.wait_ge(pv_read, u)
                    step(V.tensor_tensor(hdq, hd[:, t % 2], hd[:, t % 2], ALU.mult))
                    V.tensor_reduce(stat[:, 48:52], hdq, AX.X, ALU.add).then_inc(hn_ss, 1)
            if u < NU:
                nk = keys(UNITS[u][0])
                dve.wait_ge(pexp_done, 2 * u + 2)
                b = u % 2
                l0, l1 = stat[:, 42 + 2 * b:43 + 2 * b], stat[:, 43 + 2 * b:44 + 2 * b]
                V.reciprocal(stat[:, 46 + b:47 + b], l0)
                step(V.reciprocal(stat[:, 61:62], l1))
                step(V.scalar_tensor_tensor(stat[:, 62:63], l0, lam[:, 4:5], stat[:, 61:62], ALU.mult, ALU.mult))
                V.scalar_tensor_tensor(pexp[:, b, 0, 0:nk], pexp[:, b, 1, 0:nk], stat[:, 62:63], pexp[:, b, 0, 0:nk],
                                       ALU.mult, ALU.add).then_inc(a_ready, 1)
            if u >= 2 and UNITS[u - 2][1] == H - 1:
                t = UNITS[u - 2][0]
                dve.wait_ge(hn_rstd, 2 + t)
                V.tensor_tensor(hd[:, t % 2], hd[:, t % 2], stat[:, 52:56].unsqueeze(2).broadcast_to([P, H, HD]),
                                ALU.mult).then_inc(hm_normed, 1)
        dve.wait_ge(g1_loaded, 32)
        dve.wait_ge(xr_loaded, 16 * NT)
        dve.wait_ge(mod_loaded, 16 * 6)
        for t in range(NT + 1):
            if t < NT:
                c = min(t, 1)
                for q in range(2):
                    i = 2 * t + q
                    dve.wait_ge(o_done, i + 1)
                    step(V.tensor_tensor(mixg[:, q], PS[:, i % 4, :], g1b[:, c, q * 512:(q + 1) * 512], ALU.mult))
                    V.tensor_tensor(x1[:, t, q * 512:(q + 1) * 512], x1[:, t, q * 512:(q + 1) * 512], mixg[:, q],
                                    ALU.add).then_inc(x1_ready, 1)
            if t >= 1:
                tt = t - 1
                c = min(tt, 1)
                dve.wait_ge(n2_rstd, tt + 1)
                if tt >= 2:
                    dve.wait_ge(h2_stored[tt % 2], 16 * (tt // 2))
                    dve.wait_ge(h2_T, tt - 1)
                step(V.scalar_tensor_tensor(h2[:, tt % 2], x1[:, tt], stat[:, 16 + tt:17 + tt], mod2[:, 1, c], ALU.mult, ALU.mult))
                V.tensor_tensor(h2[:, tt % 2], h2[:, tt % 2], mod2[:, 0, c], ALU.add).then_inc(h2_ready, 1)
        dve.wait_ge(route_done, 1)
        step(V.tensor_tensor(lgt[:], PS[:, 6, 0:100].rearrange("p (t n) -> p t n", t=NT),
                             broute[:].unsqueeze(1).broadcast_to([P, NT, 20]), ALU.add))
        b4 = lambda v: v.unsqueeze(2).broadcast_to([P, NT, 4])
        prio = misc[:, 16:20].unsqueeze(1).broadcast_to([P, NT, 4])

        def first_max(src, mx, eq, val, vmax, hot):
            step(V.tensor_reduce(mx, src, AX.X, ALU.max))
            step(V.tensor_tensor(eq, src, b4(mx), ALU.is_equal))
            step(V.tensor_tensor(val, eq, prio, ALU.mult))
            step(V.tensor_reduce(vmax, val, AX.X, ALU.max))
            step(V.tensor_tensor(hot, val, b4(vmax), ALU.is_equal))

        lg = lgt[:, :, 0:4]
        first_max(lg, rs[:, 0], rt[:, 2], rt[:, 3], rs[:, 1], rt[:, 0])
        step(V.tensor_tensor(rt[:, 1], lg, b4(rs[:, 0]), ALU.subtract))
        le = lgt[:, :, 4:20].rearrange("p t (g j) -> p t g j", g=NG)
        gh = rt[:, 0].unsqueeze(3).broadcast_to([P, NT, NG, EG])
        v16 = lambda i: r16[:, i].rearrange("p t (g j) -> p t g j", g=NG)
        step(V.tensor_tensor(v16(2), le, gh, ALU.mult))
        step(V.tensor_reduce(rt[:, 4], r16[:, 2].rearrange("p t (g j) -> p t j g", g=NG), AX.X, ALU.add))
        first_max(rt[:, 4], rs[:, 3], rt[:, 5], rt[:, 6], rs[:, 4], rt[:, 7])
        step(V.scalar_tensor_tensor(rt[:, 8], rt[:, 7], -BIG, rt[:, 4], ALU.mult, ALU.add))
        first_max(rt[:, 8], rs[:, 5], rt[:, 9], rt[:, 10], rs[:, 6], rt[:, 11])
        step(V.tensor_tensor(rs[:, 2], rs[:, 5], rs[:, 3], ALU.subtract))
        dve.sem_inc(route_arg, 1)
        for j, hot in ((0, rt[:, 7]), (1, rt[:, 11])):
            last = V.tensor_tensor(v16(j), gh, hot.unsqueeze(2).broadcast_to([P, NT, NG, EG]), ALU.mult)
        step(last)
        V.tensor_tensor(ohb[:], r16[:, 0], r16[:, 1], ALU.add).then_inc(oh_ready, 1)
        dve.wait_ge(route_exp, 2)
        V.tensor_reduce(rs[:, 7], rt[:, 1], AX.X, ALU.add)
        step(V.tensor_scalar(rs[:, 8], rs[:, 2], 1.0, None, ALU.add))
        step(V.tensor_tensor(rs[:, 7], rs[:, 7], rs[:, 8], ALU.mult))
        step(V.reciprocal(rs[:, 9], rs[:, 7]))
        V.tensor_tensor(rs[:, 10], rs[:, 9], rs[:, 2], ALU.mult)
        expert = misc[:, 0:NE].unsqueeze(1).broadcast_to([P, NT, NE])
        for j in range(2):
            step(V.tensor_tensor(r16[:, 2], expert, r16[:, j], ALU.mult))
            step(V.tensor_reduce(rs[:, 14 + j], r16[:, 2], AX.X, ALU.add))
        dve.wait_ge(rank_done, 1)
        V.tensor_reduce(cnt[:, 0:1], PS[:, 7, 80:96], AX.X, ALU.max)
        rank = PS[:, 7, 0:80].rearrange("p (t e) -> p t e", e=NE)
        for j in range(2):
            step(V.tensor_tensor(r16[:, 2], rank, r16[:, j], ALU.mult))
            step(V.tensor_reduce(rs[:, 12 + j], r16[:, 2], AX.X, ALU.add))
        r2, e2, b2, s2 = (rs[:, i:i + 2] for i in (12, 14, 16, 18))
        step(V.tensor_scalar(b2, r2, float(P), None, ALU.is_ge))
        step(V.tensor_scalar(cnt[:, 1:2], cnt[:, 0:1], float(P), 1.0, ALU.is_gt, ALU.add))
        for k in range(2, ROUNDS):
            step(V.scalar_tensor_tensor(b2, r2, float(k * P), b2, ALU.is_ge, ALU.add))
            step(V.scalar_tensor_tensor(cnt[:, 1:2], cnt[:, 0:1], float(k * P), cnt[:, 1:2], ALU.is_gt, ALU.add))
        V.tensor_copy(rnd[:], cnt[:, 1:2])
        V.scalar_tensor_tensor(slot[:, 0:2], r2, float(NE), e2, ALU.mult, ALU.add)
        step(V.scalar_tensor_tensor(s2, e2, float(P), r2, ALU.mult, ALU.add))
        step(V.scalar_tensor_tensor(slot[:, 2:4], b2, float(-P), s2, ALU.mult, ALU.add))
        dve.sem_inc(slots_ready, 1)
        dve.sem_inc(rounds_ready, 1)
        n_rounds = dve.value_load(rnd[0:1, 0:1], min_val=1, max_val=ROUNDS)
        for b in range(2):
            dve.sem_inc(hid_ready[b], 1)
            dve.sem_inc(hidT_ready[b], 1)
        dve.sem_inc(y_sum, 2)
        base = n[0]
        PER_ROUND = 2 + 3 * NT
        with dve.Fori(0, n_rounds) as r:
            with dve.Fori(0, PAIRS) as q:
                it = r * PAIRS + q
                for b in range(2):
                    dve.wait_ge(sil_ready[b], it + 1)
                    V.tensor_tensor(hid[:, b], sil[:, b], PS[:, 4 + b, EH:2 * EH], ALU.mult).then_inc(hid_ready[b], 1)
                for b in range(2):
                    dve.wait_ge(hid_T[b], it + 1)
                    dve.wait_ge(dn_done[b], it + 1)
                    V.tensor_copy(hidT[:, b], PS[:, 6, 256 * b:256 * b + 256].rearrange("p (k s) -> p k s", k=2)
                                  ).then_inc(hidT_ready[b], 1)
            n[0] = 0

            def rstep(ins):
                n[0] += 1
                ins.then_inc(dstep, 1)
                dve.wait_ge(dstep, r * PER_ROUND + (base + n[0]))

            rstep(V.scalar_tensor_tensor(rs[:, 20:22], rs[:, 16:18], 0.0, rs[:, 9:11], ALU.is_equal, ALU.mult))
            rstep(V.tensor_scalar(rs[:, 16:18], rs[:, 16:18], -1.0, None, ALU.add))
            for t in range(NT):
                c = min(t, 1)
                uses = 3 - t % 2
                dve.wait_ge(pick_in[t % 2], r * (32 * uses) + 32 * (t // 2 + 1))
                y0, y1 = ypick[:, t % 2, 0], ypick[:, t % 2, 1]
                rstep(V.tensor_scalar(y0, y0, rs[:, 20, t:t + 1], None, ALU.mult))
                rstep(V.scalar_tensor_tensor(y0, y1, rs[:, 21, t:t + 1], y0, ALU.mult, ALU.add))
                rstep(V.tensor_tensor(y0, y0, g2b[:, c], ALU.mult))
                V.tensor_tensor(x1[:, t], x1[:, t], y0, ALU.add).then_inc(y_sum, 1)
            assert n[0] == PER_ROUND
            dve.wait_ge(y_sum, r * NT + (NT + 2))
        dve.sem_inc(x2_ready, 1)
        for t in range(NT):
            dve.wait_ge(fin_rstd, t + 1)
            V.scalar_tensor_tensor(x1[:, t], x1[:, t], stat[:, 16 + t:17 + t], fnorm[:], ALU.mult, ALU.mult
                                   ).then_inc(fin_ready, 1)

    @block.tensor
    def _(pe):
        mm = nc.tensor.matmul
        tr = nc.tensor.transpose

        pe.wait_ge(vec_loaded, 16 * 7)
        tr(PS[:, 7, 0:40], vrows[:], ident[0:40, 0:40]).then_inc(cols_T, 1)
        for t in range(NT):
            pe.wait_ge(xn_ready, t + 1)
            if t >= 2:
                pe.wait_ge(hraw_a, t - 1)
                pe.wait_ge(hraw_v, t - 1)
            for k in range(KD):
                last = tr(PS[:, 2 * (t % 2) + k // 4, (k % 4) * P:(k % 4 + 1) * P], xn[:, t % 2, k * P:(k + 1) * P], ident[:])
            last.then_inc(xnT_done, 1)

        def halves(ci, hf):
            pe.wait_ge(half_in[2 * (ci % 2) + hf], 16 * (ci // 2 + 1))

        def ada(n_, ci):
            if n_ >= 2:
                pe.wait_ge(ada_row, n_ - 1)
            for k in range(KD):
                if k % 4 == 0:
                    halves(ci, k // 4)
                last = mm(PS[0:2, 4 + n_ % 2, :], silc[:, k, :], ring[:, ci % 2, k, :], start=(k == 0), stop=(k == KD - 1))
            last.then_inc(ada_done, 1)

        def ada_cols(n_):
            pe.wait_ge(ada_row, n_ + 1)
            for j in range(4):
                last = tr(PS[:, 6, 2 * (4 * n_ + j):2 * (4 * n_ + j) + 2], ada_b[:, n_ % 2, j * P:(j + 1) * P], ident[0:2, 0:2])
            last.then_inc(adacol_T, 1)

        pe.wait_ge(silc_ready, 1)
        for n_ in range(4):
            ada(n_, ADA1 + n_)
            pe.wait_ge(ada_done, n_ + 1)
            pe.sem_inc(chunk_used, 1)
            if n_ >= 1:
                ada_cols(n_ - 1)
        ada_cols(3)
        pe.wait_ge(h_ready, 1)
        pe.wait_ge(small_loaded, 16 * SMALL)
        for t in range(NT):
            for k in range(KD):
                last = mm(PS[:, 7, 16 * t:16 * t + 16], hTv[:, k, t * P:(t + 1) * P], wgate[:, k, :],
                          start=(k == 0), stop=(k == KD - 1))
        last.then_inc(gate_done, 1)

        def heads_T(s, w, t, rc):
            if w in ("dk", "dq") and t > 0:
                pe.wait_ge(roped, ROPED[(w, t)])
                src = rr[:, rc % 2]
            elif w == "mk":
                pe.wait_ge(mm_evac, t + 1)
                src = mk_tok[:, t].rearrange("p h d -> p (h d)")
            else:
                pe.wait_ge(mm_evac, WIN_ORDER.index(w) * NT + t + 1)
                src = xr[:, rc % 2]
            if s >= 2:
                pe.wait_ge(win_Tevac, s - 1)
            for h in range(H):
                last = tr(PS[:, 4 + s % 2, h * P:(h + 1) * P], src[:, h * P:(h + 1) * P], ident[:])
            last.then_inc(win_T, 1)

        ROPED = {(w, t): 4 * i + t for i, w in enumerate(("dk", "dq")) for t in range(1, NT)}
        pend = None
        s = rc = 0
        for c, w in enumerate(WIN_ORDER):
            ci = WIN0 + c
            for t in range(NT):
                m = c * NT + t
                if m >= 4:
                    pe.wait_ge(mm_evac, m - 3)
                for k in range(KD):
                    if t == 0 and k % 4 == 0:
                        halves(ci, k // 4)
                    last = mm(PS[:, m % 4, :], hTv[:, k, t * P:(t + 1) * P], ring[:, ci % 2, k, :],
                              start=(k == 0), stop=(k == KD - 1))
                last.then_inc(mm_done, 1)
                if t == NT - 1:
                    pe.wait_ge(mm_done, m + 1)
                    pe.sem_inc(chunk_used, 1)
                if pend is not None:
                    heads_T(*pend)
                    pend = None
                if w in ("mk", "mq", "dk", "dq"):
                    pend = (s, w, t, rc)
                    s += 1
                    rc += w != "mk"
                if w == "mk" and t == 0:
                    pe.wait_ge(gate_tok, 1)
                    for tt in range(NT):
                        last = tr(PS[0:16, 6:8, :].rearrange("p b n -> p (b n)")[:, tt * P:(tt + 1) * P], gtok[:, tt, :], ident[:])
                    last.then_inc(gate_T, 1)
                if w == "mq" and t == 2:
                    pe.wait_ge(mendd_ready, 1)
                    for i, v in enumerate((gi, gf, ee)):
                        for d in range(2):
                            for tt in range(NT):
                                o = ((i * 2 + d) * NT + tt) * H
                                last = tr(PS[:, 6, o:o + H], v[:, d, tt * P:(tt + 1) * P], ident[0:H, 0:H])
                    last.then_inc(gcol_T, 1)
                    mm(PS[:, 7, 0:40], ones4[:], mendd[:].rearrange("p d t h -> p (d t h)"), start=True, stop=True).then_inc(mend_bc, 1)
        assert pend is None
        for n_ in range(4, 12):
            if n_ == 4:
                pe.wait_ge(win_Tevac, s)
            ada(n_, ADA2 + n_ - 4)
            pe.wait_ge(ada_done, n_ + 1)
            pe.sem_inc(chunk_used, 1)
        pe.wait_ge(state_loaded, 16)
        pe.wait_ge(coef_args, 1)
        for e in range(8):
            last = tr(PS[:, 6 + e // 4, (e % 4) * P:(e % 4 + 1) * P], sC[:, e, :], ident[:])
        last.then_inc(state_T, 1)
        pe.wait_ge(cache_loaded, 32)
        pe.wait_ge(mm_evac, NT * len(WIN_ORDER))
        for h in range(H):
            last = tr(PS[:, 0, h * P:(h + 1) * P], kc[:, h * P:(h + 1) * P], ident[:])
        last.then_inc(ck_T, 1)
        pe.wait_ge(ct0_ready, 1)
        pe.wait_ge(ck_ready, 1)
        for g, (d, t) in enumerate(MG):
            tok = slice(t * P, (t + 1) * P)
            if g >= 1:
                pe.wait_ge(w_ready, g)
                pe.wait_ge(sw_ready, g)
            mm(PS[:, 1, :], identb[:], masksb[:, d, :].unsqueeze(1).broadcast_to([P, H, P]), start=True, stop=False)
            for h in range(H):
                last = mm(PS[:, 1, h * P:(h + 1) * P], sel[:, h, :], gf[:, d, tok], start=False, stop=(h == H - 1))
            last.then_inc(mb_done, 1)
            for h in range(H):
                last = mm(PS[:, 0, h * P:(h + 1) * P], mkT[:, h, tok], mqT[:, h, tok], start=True, stop=True)
            last.then_inc(st_done, 1)
            if g < NUPD:
                pe.wait_ge(kw_ready, g + 1)
                if g >= 1:
                    pe.wait_ge(ct_ready, g)
                if 1 <= g <= 2:
                    pe.wait_ge(newC_ready, g)
                for h in range(H):
                    last = mm(PS[:, 6 + h // 2, (h % 2) * 129:(h % 2 + 1) * 129], kw[:, g % 2, h, :], mv1[:, t, h, :],
                              start=True, stop=True)
                last.then_inc(upd_done, 1)
            if g >= 1:
                pe.wait_ge(num_read, g)
            if t > 0:
                i = (g // 2) - 1
                if i > 0:
                    pe.wait_ge(ct_ready, g - 1)
                for h in range(H):
                    mm(PS[:, 4 + h // 2, (h % 2) * 129:(h % 2 + 1) * 129], mqT[:, h, tok], CT[:, d, i % 2, h, :],
                       start=True, stop=True)
            pe.wait_ge(sw_ready, g + 1)
            for h in range(H):
                last = mm(PS[:, 2 + h // 2, (h % 2) * 129:(h % 2 + 1) * 129], sw[:, g % 2, h, :], mv1[:, t, h, :],
                          start=True, stop=True)
            last.then_inc(num_done, 1)
            if g < 2:
                pe.wait_ge(ct_ready, g + 1)
                for h in range(H):
                    last = tr(PS[:, 6 + d, h * P:(h + 1) * P], CT[:, d, 1, h, 0:HD], ident[:])
                last.then_inc(newC_T, 1)
        for t in range(NT):
            pe.wait_ge(hm_normed, t + 1)
            if t >= 2:
                pe.wait_ge(mix_ready, t - 1)
            for h in range(H):
                last = tr(PS[:, 6 + t % 2, h * P:(h + 1) * P], hm[:, t, h, :], ident[:])
            last.then_inc(mix_T, 1)
        for u in range(NU + 2):
            if u < NU:
                t, h = UNITS[u]
                for m in range(2):
                    if u >= 1:
                        pe.wait_ge(pexp_done, 2 * (u - 1) + m + 1)
                    q = dqT[QK * m:QK * m + QK, h, t * P:(t + 1) * P]
                    k_ = dkT[QK * m:QK * m + QK, h]
                    if t == 0:
                        last = mm(PS[:, 2 * m, 0:P], q, k_[:, 0:CTX], start=True, stop=True)
                    else:
                        mm(PS[:, 2 * m, :], q, k_[:, CTX:T], start=True, stop=True)
                        last = mm(PS[:, 2 * m + 1, 0:PAST], q, ckT[QK * m:QK * m + QK, h], start=True, stop=True)
                    last.then_inc(sc_done, 1)
            if 1 <= u <= NU:
                t, h = UNITS[u - 1]
                nkt = keys(t) // P
                pe.wait_ge(a_ready, u)
                if u >= 2:
                    pe.wait_ge(aT_ready, u - 1)
                for kt in range(nkt):
                    last = tr(PS[:, 4 + kt // 4, (kt % 4) * P:(kt % 4 + 1) * P],
                              pexp[:, (u - 1) % 2, 0, kt * P:(kt + 1) * P], ident[:])
                last.then_inc(a_T, 1)
                pe.wait_ge(aT_ready, u)
                if u == 1:
                    pe.wait_ge(mix_ready, NT)
                if u > H:
                    pe.wait_ge(pv_read, u - H)
                for kt in range(nkt):
                    v = dv_tok[:, 0, h, :] if t == 0 else (vc[:, h, :] if kt == 4 else dv_tok[:, 1 + kt, h, :])
                    last = mm(PS[:, 6, h * HD:(h + 1) * HD], aT[:, (u - 1) % 2, kt, :], v, start=(kt == 0), stop=(kt == nkt - 1))
                last.then_inc(pv_done, 1)
            if u >= 2 and UNITS[u - 2][1] == H - 1:
                t = UNITS[u - 2][0]
                pe.wait_ge(hm_normed, NT + t + 1)
                if t >= 1:
                    pe.wait_ge(mix_ready, NT + t)
                for hh in range(H):
                    last = tr(PS[:, 7, hh * P:(hh + 1) * P], hd[:, t % 2, hh, :], ident[:])
                last.then_inc(mix_T, 1)
        pe.wait_ge(mix_ready, 2 * NT)
        for hf in range(2):
            halves(WOUT, hf)
            halves(WOUT + 1, hf)
        for t in range(NT + 1):
            if t < NT:
                for q in range(2):
                    i = 2 * t + q
                    if i >= 4:
                        pe.wait_ge(x1_ready, i - 3)
                    for k in range(KD):
                        last = mm(PS[:, i % 4, :], hTv[:, k, t * P:(t + 1) * P], ring[:, (WOUT + q) % 2, k, :],
                                  start=(k == 0), stop=(k == KD - 1))
                    last.then_inc(o_done, 1)
            if t >= 1:
                tt = t - 1
                pe.wait_ge(h2_ready, tt + 1)
                if tt >= 1:
                    pe.wait_ge(h2T_ready, tt)
                for k in range(KD):
                    last = tr(PS[:, 4 + k // 4, (k % 4) * P:(k % 4 + 1) * P], h2[:, tt % 2, k * P:(k + 1) * P], ident[:])
                last.then_inc(h2_T, 1)
                pe.wait_ge(h2T_ready, tt + 1)
                for k in range(KD):
                    last = mm(PS[:, 6, 20 * tt:20 * tt + 20], hTv[:, k, tt * P:(tt + 1) * P], wroute[:, k, :],
                              start=(k == 0), stop=(k == KD - 1))
        last.then_inc(route_done, 1)
        pe.wait_ge(oh_ready, 1)
        for t in range(NT):
            for j in range(t + 1):
                mm(PS[:, 7, NE * t:NE * t + NE], masksb[:, 2 if j == t else 3, :], ohb[:, j, :], start=(j == 0), stop=(j == t))
        for j in range(NT):
            last = mm(PS[:, 7, 80:96], masksb[:, 3, :], ohb[:, j, :], start=(j == 0), stop=(j == NT - 1))
        last.then_inc(rank_done, 1)
        pe.wait_ge(rounds_ready, 1)
        n_rounds = pe.value_load(rnd[0:1, 0:1], min_val=1, max_val=ROUNDS)
        for b in range(2):
            pe.sem_inc(xg_T[b], 1)
            pe.sem_inc(gu_done[b], 1)
            pe.sem_inc(dn_done[b], 1)
        with pe.Fori(0, n_rounds * PAIRS) as it:
            for b in range(2):
                pe.wait_ge(xg_in[b], 16 * it + 16)
                pe.wait_ge(yo_ready[b], it + 1)
                for k in range(KD):
                    last = tr(PS[:, 2 * b + k // 4, (k % 4) * P:(k % 4 + 1) * P], xg[:, b, k * P:(k + 1) * P], ident[:])
                last.then_inc(xg_T[b], 1)
            for b in range(2):
                pe.wait_ge(xgT_ready[b], it + 1)
                pe.wait_ge(wg_in[b], 16 * it + 16)
                pe.wait_ge(hid_ready[b], it + 1)
                for k in range(KD):
                    last = mm(PS[:, 4 + b, :], xgT[:, b, k, :], gub[b][:, k, :], start=(k == 0), stop=(k == KD - 1))
                last.then_inc(gu_done[b], 1)
                pe.wait_ge(gu_done[b], it + 2)
                pe.sem_inc(wg_used[b], 1)
            for b in range(2):
                pe.wait_ge(hid_ready[b], it + 2)
                pe.wait_ge(hidT_ready[b], it + 1)
                for k in range(2):
                    last = tr(PS[:, 6, 256 * b + k * P:256 * b + (k + 1) * P], hid[:, b, k * P:(k + 1) * P], ident[:])
                last.then_inc(hid_T[b], 1)
                pe.wait_ge(hidT_ready[b], it + 2)
                pe.wait_ge(wd_in[b], 16 * it + 16)
                for q in range(2):
                    for k in range(2):
                        last = mm(PS[:, 2 * b + q, :], hidT[:, b, k, :], dnb[b][:, k, q * 512:(q + 1) * 512],
                                  start=(k == 0), stop=(k == 1))
                last.then_inc(dn_done[b], 1)
                pe.wait_ge(dn_done[b], it + 2)
                pe.sem_inc(wd_used[b], 1)


_INS = ["x_prompt", "x_sample", "cache_k", "cache_v", "state_C", "state_n", "state_m", "c", "c_ctx", "w_ada", "b_ada",
        "norm_mix", "norm_ffn", "w_in", "b_gate", "mlstm_norm", "diff_norm", "diff_lambda", "w_out", "w_route_group",
        "b_route_group", "w_route_expert", "b_route_expert", "w_gate_up", "w_down", "final_norm"]
_OUTS = {"y_prompt": (1, CTX, D), "y_sample": (1, LAT, D), "new_k": (1, 1, CTX, H, 2, QK), "new_v": (1, 1, CTX, H, HD),
         "new_C": (1, 1, 2, H, HD, HD), "new_n": (1, 1, 2, H, HD), "new_m": (1, 1, 2, H)}
_SCRATCH = {"mod": ((2, 4 * D), F32), "h2": ((T, D), F32), "y": ((NE * P, D), F32), "ids": ((ROUNDS * NE * P, 1), U32)}


def kernel(**inputs):
    import concourse.bacc as _bacc
    from concourse.bass_utils import run_bass_kernel_spmd as _run

    nc = _bacc.Bacc("TRN2", target_bir_lowering=False, num_devices=1)
    arrays = {k: np.ascontiguousarray(inputs[k]) for k in _INS}
    arrays.update(shape_constants())
    a = {k: nc.dram_tensor(f"in_{k}", v.shape, mybir.dt.from_np(v.dtype), kind="ExternalInput").ap() for k, v in arrays.items()}
    o = {k: nc.dram_tensor(f"out_{k}", v, F32, kind="ExternalOutput").ap() for k, v in _OUTS.items()}
    s = {k: nc.dram_tensor(f"scratch_{k}", v, dt, kind="Internal").ap() for k, (v, dt) in _SCRATCH.items()}
    build(nc, a, o, s)
    r = _run(nc, [{f"in_{k}": v for k, v in arrays.items()}], core_ids=[0])
    return tuple(r.results[0][f"out_{k}"] for k in _OUTS)
```

```python
import math
from contextlib import ExitStack

import numpy as np

import concourse.bass as bass
from concourse import mybir

F32 = mybir.dt.float32
BF16 = mybir.dt.bfloat16
U32 = mybir.dt.uint32
I32 = mybir.dt.int32
ALU = mybir.AluOpType
ACT = mybir.ActivationFunctionType
AX = mybir.AxisListType

P = 128
D = 1024
KD = D // P
CTX = 128
LAT = 512
T = CTX + LAT
NT = T // P
PAST = 128
H = 4
HD = 128
QK = 64
EPS = 1e-6
GRID_W = 64
THETA = 10000.0
LAM_INIT = 0.8 - 0.6 * math.exp(0.0)
OFF = {"mq": 0, "mk": 512, "mv": 1024, "mo": 1536, "gate": 2048, "dq": 2064, "dk": 2576, "dv": 3088}
NG = 4
EG = 4
NE = NG * EG
EH = D // 4
ROUNDS = T // P
BIG = 2.0 ** 99
WIN_ORDER = ["mk", "mq", "mv", "dk", "dq", "dv", "mo"]
ALONE = 3
SMALL = 16
CHUNKS = ([("ada", n * 512) for n in range(4)] + [(w, OFF[w]) for w in WIN_ORDER]
          + [("ada", n * 512) for n in range(4, 12)] + [("out", 0), ("out", 512)])
ADA1, WIN0, ADA2, WOUT = 0, 4, 11, 19


def shape_constants():
    ident = np.eye(P, dtype=np.float32)
    s, t = np.arange(P)[:, None], np.arange(P)[None, :]
    masks = np.stack([np.where(s > t, BIG, 0.0), np.where(s < t, BIG, 0.0),
                      np.where(s < t, 1.0, 0.0), np.ones((P, P))], 1).astype(np.float32)
    eye4 = np.tile(np.eye(H, dtype=np.float32)[:, None, :], (1, NT, 1))
    half = QK // 4
    freqs = THETA ** (-np.arange(half, dtype=np.float32) / half)
    tok = np.arange(LAT)
    ang = np.stack([(tok // GRID_W)[:, None] * freqs, (tok % GRID_W)[:, None] * freqs], 1).astype(np.float32)
    cos = np.stack([np.cos(ang), np.cos(ang)], 2)
    sin = np.stack([-np.sin(ang), np.sin(ang)], 2)
    rope = np.stack([cos, sin], 0).reshape(2, LAT // P, P, QK).transpose(2, 0, 1, 3).astype(np.float32)
    misc = np.zeros((P, 64), np.float32)
    misc[:, 0:NE] = np.arange(NE)
    misc[:, 16:32] = np.tile(EG - np.arange(EG), NG)
    misc[:, 32:37] = np.arange(NT)[None, :] * P + np.arange(P)[:, None]
    return {"c_ident": ident, "c_masks": masks, "c_eye4": eye4,
            "c_rope": np.ascontiguousarray(rope), "c_misc": misc}


def build(nc, a, out, scratch):
    with ExitStack() as ctx:
        build_body(nc, ctx, a, out, scratch)


def build_body(nc, ctx, a, out, scratch):
    def sb(name, shape, dt=F32):
        return ctx.enter_context(nc.sbuf_tensor(name, shape, dt))

    def sem(name):
        return ctx.enter_context(nc.semaphore(name))

    hT = sb("hT", [P, KD * T])
    PR = sb("PR", [P, 20500])
    HM = sb("HM", [P, NT * 512])
    RING = sb("RING", [P, 2 * KD * 512])
    TMP = sb("TMP", [P, 13076])
    PS = ctx.enter_context(nc.psum_tensor("PS", [P, 8, 512], F32))

    ident = sb("ident", [P, P])
    identb = sb("identb", [P, P], BF16)
    onesf = sb("onesf", [P, P])
    masksb = sb("masksb", [P, 4, P], BF16)
    ones4 = sb("ones4", [H, P])
    eye4 = sb("eye4", [H, NT, H])
    rope = sb("rope", [P, 2, 4, QK])
    misc = sb("misc", [P, 64])
    fnorm = sb("fnorm", [P, D])
    wgate = sb("wgate", [P, KD, 16])
    wroute = sb("wroute", [P, KD, 20])
    vrows = sb("vrows", [40, P])
    cols = sb("cols", [P, 40])
    silc = sb("silc", [P, KD, 2])
    modc = sb("modc", [P, 16, 2])
    lam = sb("lam", [P, 8])
    bgate = sb("bgate", [16, 1])
    broute = sb("broute", [20, 1])
    lgT = sb("lgT", [20, P])
    stat = sb("stat", [P, 64])
    sm_in = sb("sm_in", [H, 2])
    m0b = sb("m0b", [P, 2, H])
    mendd = sb("mendd", [H, 2, NT, H])
    mend = sb("mend", [P, 2, NT, H])
    mprev = sb("mprev", [P, 2, NT, H])
    gcol = sb("gcol", [P, 3, 2, NT, H])
    coef = sb("coef", [P, 4, 2, NT, H])
    nout = sb("nout", [P, 2, H])
    newm = sb("newm", [H, 2])

    x_in = PR[:, 15380:20500].rearrange("p (t d) -> p t d", t=NT)
    xn = PR[:, 10260:12308].rearrange("p (b d) -> p b d", b=2)
    junk = PR[:, 12820:13844]
    hTv = hT[:, :].rearrange("p (k t) -> p k t", k=KD)
    mk_tok = PR[:, 0:2560].rearrange("p (t h d) -> p t h d", t=NT, h=H)
    mv1 = PR[:, 2560:5140].rearrange("p (t h d) -> p t h d", t=NT, h=H)
    sgo = PR[:, 5140:7700].rearrange("p (t d) -> p t d", t=NT)
    dv_tok = PR[:, 7700:10260].rearrange("p (t h d) -> p t h d", t=NT, h=H)
    mqT, mkT, dqT, dkT = (PR[:, 10260 + 2560 * i:12820 + 2560 * i].rearrange("p (h t) -> p h t", h=H)
                          for i in range(4))
    hm = HM[:, :].rearrange("p (t h d) -> p t h d", t=NT, h=H)
    ada_b1 = TMP[0:2, 4628:5652].rearrange("p (b n) -> p b n", b=2)
    ada_b2 = TMP[0:2, 11796:12820].rearrange("p (b n) -> p b n", b=2)
    ada_g = fnorm[0:2, :]
    ring = RING[:, :].rearrange("p (b k n) -> p b k n", b=2, k=KD)

    gi = TMP[0:H, 0:1280].rearrange("p (d t) -> p d t", d=2)
    ee = TMP[0:H, 1280:2560].rearrange("p (d t) -> p d t", d=2)
    gf = TMP[0:H, 11796:13076].rearrange("p (d t) -> p d t", d=2)
    mdiag = TMP[0:H, 11284:11796].rearrange("p (h t) -> p h t", h=H)
    masks = TMP[:, 11284:11796].rearrange("p (m t) -> p m t", m=4)
    wexp = TMP[:, 0:1024].rearrange("p (b h t) -> p b h t", b=2, h=H)
    sw = TMP[:, 1024:2048].rearrange("p (b h t) -> p b h t", b=2, h=H)
    CT = TMP[:, 2048:4112].rearrange("p (d b h v) -> p d b h v", d=2, b=2, h=H)
    num = TMP[:, 4112:4628].rearrange("p (h v) -> p h v", h=H)
    lamb = TMP[:, 4112:4368].rearrange("p (i k) -> p i k", i=4)
    kw = TMP[:, 4628:5652].rearrange("p (b h k) -> p b h k", b=2, h=H)
    newC = TMP[:, 5652:6676].rearrange("p (e k) -> p e k", e=8)
    sC = newC
    xr = TMP[:, 6676:7700].rearrange("p (b n) -> p b n", b=2)
    xs = TMP[:, 7700:8724].rearrange("p (b n) -> p b n", b=2)
    rr = TMP[:, 8724:9748].rearrange("p (b n) -> p b n", b=2)
    grow = TMP[0:16, 7700:8340]
    gzero = TMP[0:H, 8724:9236]
    kc = TMP[:, 9748:10260]
    vc = TMP[:, 10260:10772].rearrange("p (h d) -> p h d", h=H)
    ckT = TMP[:, 10772:11284].rearrange("p (h t) -> p h t", h=H)
    pexp = TMP[:, 0:2560].rearrange("p (b m k) -> p b m k", b=2, m=2)
    aT = TMP[:, 2560:7680].rearrange("p (b t q) -> p b t q", b=2, t=5)
    osq = TMP[:, 7680:8320]
    aTc = TMP[:, 8320:8576].rearrange("p (b q) -> p b q", b=2)
    octx = TMP[:, 8576:8704]
    scores = PS[:, 0:3, :].rearrange("p b n -> p (b n)")[:, 0:2 * (LAT + PAST)].rearrange("p (m k) -> p m k", m=2)
    aT_ps = PS[:, 3:5, :].rearrange("p b n -> p (b n)")[:, 0:LAT + PAST]
    x1 = TMP[:, 0:5120].rearrange("p (t d) -> p t d", t=NT)
    mod2 = TMP[:, 5120:9216].rearrange("p (s c d) -> p s c d", s=2, c=2)
    g1b = HM[:, 0:2048].rearrange("p (c d) -> p c d", c=2)
    g2b = PR[:, 18432:20480].rearrange("p (c d) -> p c d", c=2)
    h2 = PR[:, 12288:14336].rearrange("p (b d) -> p b d", b=2)
    junkn = PR[:, 14336:15360]
    mixg = PR[:, 15380:16404].rearrange("p (b n) -> p b n", b=2)
    hsq = PR[:, 10260:12820].rearrange("p (t h d) -> p t h d", t=NT, d=HD)
    gub = [PR[:, 6144 * b:6144 * b + 4096].rearrange("p (k n) -> p k n", k=KD) for b in range(2)]
    dnb = [PR[:, 6144 * b + 4096:6144 * b + 6144].rearrange("p (k n) -> p k n", k=2) for b in range(2)]
    xg = RING[:, 0:2048].rearrange("p (b d) -> p b d", b=2)
    xgT = RING[:, 2048:4096].rearrange("p (b k s) -> p b k s", b=2, k=KD)
    hid = RING[:, 4096:4608].rearrange("p (b n) -> p b n", b=2)
    hidT = RING[:, 4608:5120].rearrange("p (b k s) -> p b k s", b=2, k=2)
    sil = RING[:, 5120:5632].rearrange("p (b n) -> p b n", b=2)
    yo = RING[:, 5632:7680].rearrange("p (b d) -> p b d", b=2)
    ypick = hT[:, 0:4096].rearrange("p (b j d) -> p b j d", b=2, j=2)

    lgt = TMP[:, 9216:9316].rearrange("p (t n) -> p t n", t=NT)
    rt = TMP[:, 9316:9556].rearrange("p (i t n) -> p i t n", i=12, t=NT)
    rs = TMP[:, 9556:9676].rearrange("p (i t) -> p i t", i=24)
    r16 = TMP[:, 9676:9996].rearrange("p (i t n) -> p i t n", i=4, t=NT)
    ohb = sb("ohb", [P, NT, NE], BF16)
    slot = sb("slot", [P, 4, NT], U32)
    tokid = sb("tokid", [P, NT], U32)
    idall = sb("idall", [P, NE], U32)
    idp = sb("idp", [P, 2], U32)
    cnt = sb("cnt", [P, 4])
    rnd = sb("rnd", [P, 1], I32)
    zid = sb("zid", [P, ROUNDS * NE], U32)

    x_loaded = [sem(f"x_loaded{t}") for t in range(NT)]
    vec_loaded = sem("vec_loaded")
    small_loaded = sem("small_loaded")
    cache_loaded = sem("cache_loaded")
    bias_loaded = [sem(f"bias_loaded{b}") for b in range(2)]
    bias2_loaded = [sem(f"bias2_loaded{b}") for b in range(2)]
    row_stored = sem("row_stored")
    half_in = [sem(f"half_in{i}") for i in range(4)]
    consts_ready = sem("consts_ready")
    cols_T = sem("cols_T")
    cols_ready = sem("cols_ready")
    silc_ready = sem("silc_ready")
    rstd_ready = sem("rstd_ready")
    xn_ready = sem("xn_ready")
    xnT_done = sem("xnT_done")
    hraw_a = sem("hraw_a")
    hraw_v = sem("hraw_v")
    ada_done = sem("ada_done")
    ada_row = sem("ada_row")
    adacol_T = sem("adacol_T")
    h_ready = sem("h_ready")
    gate_done = sem("gate_done")
    gate_rows = sem("gate_rows")
    gate_split = sem("gate_split")
    nabs_f = sem("nabs_f")
    softp = sem("softp")
    mendd_ready = sem("mendd_ready")
    mend_bc = sem("mend_bc")
    coef_args = sem("coef_args")
    coef_ready = sem("coef_ready")
    mm_done = sem("mm_done")
    mm_evac = sem("mm_evac")
    win_T = sem("win_T")
    win_Tevac = sem("win_Tevac")
    roped = sem("roped")
    state_T = sem("state_T")
    ct0_ready = sem("ct0_ready")
    kw_ready = sem("kw_ready")
    mdiag_ready = sem("mdiag_ready")
    mb_done = sem("mb_done")
    int_done = sem("int_done")
    int_read = sem("int_read")
    w_ready = sem("w_ready")
    st_done = sem("st_done")
    sw_ready = sem("sw_ready")
    upd_done = sem("upd_done")
    ct_ready = sem("ct_ready")
    num_done = sem("num_done")
    num_read = sem("num_read")
    hm_ready = sem("hm_ready")
    newC_T = sem("newC_T")
    newC_ready = sem("newC_ready")
    outs = sem("outs")
    sg_ready = sem("sg_ready")
    hn_sq = sem("hn_sq")
    hn_ss = sem("hn_ss")
    hn_rstd = sem("hn_rstd")
    hm_normed = sem("hm_normed")
    mix_T = sem("mix_T")
    mix_ready = sem("mix_ready")
    ck_T = sem("ck_T")
    ck_ready = sem("ck_ready")
    osq_ready = sem("osq_ready")
    oss_done = sem("oss_done")
    pvc_done = sem("pvc_done")
    ossc_done = sem("ossc_done")
    ossc_read = sem("ossc_read")
    orstd = sem("orstd")
    omix = sem("omix")
    sc_done = sem("sc_done")
    smax = sem("smax")
    pexp_done = sem("pexp_done")
    a_ready = sem("a_ready")
    a_T = sem("a_T")
    aT_ready = sem("aT_ready")
    pv_done = sem("pv_done")
    lam_args = sem("lam_args")
    lam_exp = sem("lam_exp")
    dstep = sem("dstep")
    astep = sem("astep")
    pstep = sem("pstep")
    mod_loaded = sem("mod_loaded")
    g1_loaded = sem("g1_loaded")
    g2_loaded = sem("g2_loaded")
    o_done = sem("o_done")
    x1_ready = sem("x1_ready")
    n2_rstd = sem("n2_rstd")
    h2_ready = sem("h2_ready")
    h2_stored = [sem(f"h2_stored{b}") for b in range(2)]
    h2_T = sem("h2_T")
    h2T_ready = sem("h2T_ready")
    logT = sem("logT")
    logT_read = sem("logT_read")
    route_done = sem("route_done")
    route_exp = sem("route_exp")
    route_arg = sem("route_arg")
    oh_ready = sem("oh_ready")
    rank_done = sem("rank_done")
    slots_ready = sem("slots_ready")
    rounds_ready = sem("rounds_ready")
    zid_stored = sem("zid_stored")
    ids_stored = sem("ids_stored")
    idall_in = sem("idall_in")
    idp_ready = sem("idp_ready")
    wg_in = [sem(f"wg_in{b}") for b in range(2)]
    wd_in = [sem(f"wd_in{b}") for b in range(2)]
    xg_in = [sem(f"xg_in{b}") for b in range(2)]
    xg_T = [sem(f"xg_T{b}") for b in range(2)]
    xgT_ready = [sem(f"xgT_ready{b}") for b in range(2)]
    gu_done = [sem(f"gu_done{b}") for b in range(2)]
    sil_ready = [sem(f"sil_ready{b}") for b in range(2)]
    hid_ready = [sem(f"hid_ready{b}") for b in range(2)]
    hid_T = [sem(f"hid_T{b}") for b in range(2)]
    hidT_ready = [sem(f"hidT_ready{b}") for b in range(2)]
    dn_done = [sem(f"dn_done{b}") for b in range(2)]
    yo_ready = [sem(f"yo_ready{b}") for b in range(2)]
    yo_stored = [sem(f"yo_stored{b}") for b in range(2)]
    pool_turn = sem("pool_turn")
    pick_in = [sem(f"pick_in{b}") for b in range(2)]
    pick_w = sem("pick_w")
    y_scaled = sem("y_scaled")
    y_sum = sem("y_sum")
    fnorm_loaded = sem("fnorm_loaded")
    eps_ready = sem("eps_ready")
    x2_ready = sem("x2_ready")
    fin_rstd = sem("fin_rstd")
    fin_ln = sem("fin_ln")
    fin_ready = sem("fin_ready")

    block = ctx.enter_context(nc.Block())

    T_NO = {}
    for m_ in range(NT * len(WIN_ORDER)):
        if WIN_ORDER[m_ // NT] in ("mk", "mq", "dk", "dq"):
            T_NO[m_] = len(T_NO)
    MG = [(0, 0), (1, 0), (0, 1), (1, 4), (0, 2), (1, 3), (0, 3), (1, 2), (0, 4), (1, 1)]
    NMG = len(MG)
    NUPD = NMG - 2
    UNITS = [(h, j) for h in range(H) for j in range(NT)]
    NU = len(UNITS)

    def ada_step(n_):
        q = 2 * (n_ - 4) + 1
        return (q // 4) * NT + 1 + q % 4

    MIX_STEPS = [NT + 1] + [NT + 3 + i for i in range(NT - 1)]

    def mix_bank(t):
        return PS[:, 7, :]
    PAIRS = NE // 2
    ADA2_N = list(range(4, 12))

    def keys(t):
        return P if t == 0 else LAT + PAST

    w_dram = {"ada": a["w_ada"][0], "out": a["w_out"][0]}

    @block.sync
    def _(sp):
        for lo, hi, src in ((0, 8, a["c_ctx"]), (8, 16, a["c"][0]), (16, 24, a["norm_mix"][0]),
                            (24, 28, a["mlstm_norm"][0]), (28, 32, a["diff_norm"][0])):
            sp.dma_start(vrows[lo:hi, :], src.rearrange("(k p) -> k p", p=P)).then_inc(vec_loaded, 16)
        sp.dma_start(vrows[32:40, :], a["state_n"][0, 0].rearrange("d h k -> (d h) k")).then_inc(vec_loaded, 16)
        sp.dma_start(ident[:], a["c_ident"]).then_inc(vec_loaded, 16)
        def load_chunk(ci):
            kind, col = CHUNKS[ci]
            w = w_dram.get(kind, a["w_in"][0]).rearrange("(h k p) n -> h p k n", h=2, p=P)
            for hf in range(2):
                sp.dma_start(ring[:, ci % 2, 4 * hf:4 * hf + 4, :],
                             w[hf, :, :, col:col + 512]).then_inc(half_in[2 * (ci % 2) + hf], 16)

        load_chunk(0)
        for t in range(NT):
            src = a["x_prompt"][0] if t == 0 else a["x_sample"][0, (t - 1) * P:t * P, :]
            sp.dma_start(x_in[:, t, :], src).then_inc(x_loaded[t], 16)
        load_chunk(1)
        for ci in range(2, len(CHUNKS)):
            kind2, col2 = CHUNKS[ci - 2]
            if kind2 == "ada":
                sp.wait_ge(ada_done, col2 // 512 + 1)
            else:
                sp.wait_ge(mm_done, NT * (WIN_ORDER.index(kind2) + 1))
            load_chunk(ci)
        rows = scratch["mod"]
        sp.wait_ge(mix_ready, NT)
        sp.wait_ge(row_stored, 16 * 2)
        for c in range(2):
            sp.dma_start(g1b[:, c, :], rows[c, 0:D].partition_broadcast(P)).then_inc(g1_loaded, 16)
        sp.wait_ge(outs, 16 * 5)
        sp.wait_ge(row_stored, 16 * 8)
        for c in range(2):
            sp.dma_start(g2b[:, c, :], rows[c, 3 * D:4 * D].partition_broadcast(P)).then_inc(g2_loaded, 16)
        sp.wait_ge(omix, H)
        for t in range(NT):
            src = a["x_prompt"][0] if t == 0 else a["x_sample"][0, (t - 1) * P:t * P, :]
            sp.dma_start(x1[:, t, :], src).then_inc(x_loaded[t], 16)
            if t == 0:
                for s in range(2):
                    for c in range(2):
                        sp.dma_start(mod2[:, s, c, :],
                                     rows[c, D * (1 + s):D * (2 + s)].partition_broadcast(P)).then_inc(mod_loaded, 16)
        sp.dma_start(fnorm[:], a["final_norm"].partition_broadcast(P)).then_inc(fnorm_loaded, 16)
        w_gu = a["w_gate_up"][0].rearrange("e (k p) n -> p e k n", p=P)
        w_dn = a["w_down"][0].rearrange("e (k p) n -> p e k n", p=P)
        for b in range(2):
            sp.dma_start(gub[b], w_gu[:, b]).then_inc(wg_in[b], 16)
            sp.dma_start(dnb[b], w_dn[:, b]).then_inc(wd_in[b], 16)
        sp.wait_ge(rounds_ready, 1)
        n_rounds = sp.value_load(rnd[0:1, 0:1], min_val=1, max_val=ROUNDS)
        with sp.Fori(1, n_rounds * PAIRS) as it:
            first = (it % PAIRS) * 2
            for b in range(2):
                sp.wait_ge(gu_done[b], it + 1)
                sp.dma_start(gub[b], w_gu[:, bass.ds(first + b, 1)].rearrange("p e k n -> p (e k) n")
                             ).then_inc(wg_in[b], 16)
                sp.wait_ge(dn_done[b], it + 1)
                sp.dma_start(dnb[b], w_dn[:, bass.ds(first + b, 1)].rearrange("p e k n -> p (e k) n")
                             ).then_inc(wd_in[b], 16)
        for t in range(NT):
            sp.wait_ge(fin_ready, t + 1)
            dst = out["y_prompt"][0] if t == 0 else out["y_sample"][0, (t - 1) * P:t * P, :]
            sp.dma_start(dst, x1[:, t, :]).then_inc(outs, 16)
        sp.wait_ge(outs, 16 * (NT + 5))

    @block.gpsimd
    def _(pool):
        n = [0]

        def step(ins):
            n[0] += 1
            ins.then_inc(pstep, 1)
            pool.wait_ge(pstep, n[0])

        small = [(masks, a["c_masks"]), (onesf[:], a["c_masks"][:, 3]), (eye4[:], a["c_eye4"]),
                 (rope[:], a["c_rope"]), (misc[:], a["c_misc"]),
                 (wgate[:], a["w_in"][0].rearrange("(k p) n -> p k n", p=P)[:, :, OFF["gate"]:OFF["gate"] + 16]),
                 (wroute[:, :, 0:4], a["w_route_group"][0].rearrange("(k p) n -> p k n", p=P)),
                 (wroute[:, :, 4:20], a["w_route_expert"][0].rearrange("(k p) n -> p k n", p=P)),
                 (bgate[:], a["b_gate"][0].unsqueeze(1)),
                 (broute[0:4], a["b_route_group"][0].unsqueeze(1)),
                 (broute[4:20], a["b_route_expert"][0].unsqueeze(1)),
                 (lamb, a["diff_lambda"][0].partition_broadcast(P)),
                 (sC, a["state_C"][0, 0].rearrange("d h v k -> v (d h) k")),
                 (sm_in[:], a["state_m"][0, 0].rearrange("d h -> h d")),
                 (m0b[:], a["state_m"][0, 0].partition_broadcast(P)),
                 (ada_g, a["norm_ffn"][0].partition_broadcast(2))]
        bias = a["b_ada"][0]
        for c in range(2):
            pool.dma_start(ada_b1[:, c, :], bias[c * 512:(c + 1) * 512].partition_broadcast(2)).then_inc(bias_loaded[c], 16)
        assert len(small) == SMALL
        for dst, src in small:
            pool.dma_start(dst, src, allow_slow_non_contiguous=dst.shape == (H, 2)).then_inc(small_loaded, 16)
        nc.gpsimd.memset(zid[:], 0).then_inc(consts_ready, 1)
        nc.gpsimd.memset(ones4[:], 1.0).then_inc(consts_ready, 1)
        pool.wait_ge(consts_ready, 2)
        pool.dma_start(scratch["ids"].rearrange("(p n) o -> p (n o)", p=P), zid[:]).then_inc(zid_stored, 16)
        for n_ in (2, 3):
            pool.wait_ge(adacol_T, n_ - 1)
            pool.dma_start(ada_b1[:, n_ % 2, :], bias[n_ * 512:(n_ + 1) * 512].partition_broadcast(2)
                           ).then_inc(bias_loaded[n_ % 2], 16)
        pool.wait_ge(gate_rows, 1)
        for g, dst in enumerate((gi[:, 0, :], gf[:, 0, :], gi[:, 1, :], gf[:, 1, :])):
            pool.dma_start(dst, grow[4 * g:4 * g + 4, :]).then_inc(gate_split, 16)
        pool.dma_start(kc, a["cache_k"][0, 0].rearrange("t h m d -> t (h m d)")).then_inc(cache_loaded, 16)
        pool.dma_start(vc, a["cache_v"][0, 0]).then_inc(cache_loaded, 16)
        pool.wait_ge(coef_ready, 1)
        pool.wait_ge(mm_evac, NT)
        pool.wait_ge(coef_args, 1)
        for g, (d, t) in enumerate(MG):
            if g >= 1:
                pool.wait_ge(mb_done, g)
            nc.gpsimd.tensor_tensor(mdiag, gf[:, d, t * P:(t + 1) * P].unsqueeze(1).broadcast_to([H, H, P]),
                                    eye4[:, 0, :].unsqueeze(2).broadcast_to([H, H, P]), ALU.mult).then_inc(mdiag_ready, 1)
            if g >= NUPD:
                continue
            if g >= 2:
                pool.wait_ge(upd_done, g - 1)
            nc.gpsimd.tensor_tensor(kw[:, g % 2], mk_tok[:, t], coef[:, 0, d, t, :].unsqueeze(2).broadcast_to([P, H, HD]),
                                    ALU.mult).then_inc(kw_ready, 1)
        pool.wait_ge(hm_ready, 1)
        for t in range(NT):
            nc.gpsimd.tensor_tensor(hsq[:, t], hm[:, t], hm[:, t], ALU.mult).then_inc(hn_sq, 1)
        for t in range(NT):
            if t == 0:
                pool.wait_ge(hn_rstd, 1)
            if t == NT - 1:
                pool.wait_ge(sg_ready, 1)
            rb_ = stat[:, 20 + 4 * t:24 + 4 * t].unsqueeze(2).broadcast_to([P, H, HD])
            step(nc.gpsimd.tensor_tensor(hm[:, t], hm[:, t], rb_, ALU.mult))
            nc.gpsimd.tensor_tensor(hm[:, t], hm[:, t], sgo[:, t].rearrange("p (h d) -> p h d", h=H),
                                    ALU.mult).then_inc(hm_normed, 1)
        pool.wait_ge(zid_stored, 16)
        for t in range(NT):
            pool.wait_ge(slots_ready, t + 1)
            for j in range(2):
                pool.indirect_dma_start(out=scratch["ids"], out_offset=bass.IndirectOffsetOnAxis(ap=slot[:, j, t:t + 1], axis=0),
                                        in_=tokid[:, t:t + 1], in_offset=None).then_inc(ids_stored, 16)
        pool.wait_ge(ids_stored, 16 * 2 * NT)
        pool.wait_ge(h2_stored[0], 16 * 3)
        pool.wait_ge(h2_stored[1], 16 * 2)
        pool.wait_ge(rounds_ready, 1)
        n_rounds = pool.value_load(rnd[0:1, 0:1], min_val=1, max_val=ROUNDS)
        with pool.Fori(0, n_rounds) as r:
            pool.dma_start(idall[:], scratch["ids"][bass.ds(r * (P * NE), P * NE), :].rearrange("(p e) o -> p (e o)", e=NE)
                           ).then_inc(idall_in, 16)
            pool.wait_ge(idall_in, 16 * (r + 1))
            pool.sem_inc(pool_turn, 1)
            with pool.Fori(0, PAIRS) as q:
                it = r * PAIRS + q
                for b in range(2):
                    pool.wait_ge(xg_T[b], it + 1)
                nc.gpsimd.tensor_copy(idp[:], idall[:, bass.ds(q * 2, 2)]).then_inc(idp_ready, 1)
                pool.wait_ge(idp_ready, it + 1)
                pool.sem_inc(pool_turn, 1)
                for b in range(2):
                    pool.indirect_dma_start(out=xg[:, b, :], out_offset=None, in_=scratch["h2"],
                                            in_offset=bass.IndirectOffsetOnAxis(ap=idp[:, b:b + 1], axis=0)
                                            ).then_inc(xg_in[b], 16)
            for b in range(2):
                pool.wait_ge(yo_stored[b], r * (PAIRS * 16) + (PAIRS * 16 + 16))
            for t in range(NT):
                pool.wait_ge(y_sum, r * NT + (2 if t == 0 else t if t == 1 else t + 1))
                pool.sem_inc(pool_turn, 1)
                for j in range(2):
                    pool.indirect_dma_start(out=ypick[:, t % 2, j, :], out_offset=None, in_=scratch["y"],
                                            in_offset=bass.IndirectOffsetOnAxis(ap=slot[:, 2 + j, t:t + 1], axis=0)
                                            ).then_inc(pick_in[t % 2], 16)
            for b in range(2):
                pool.wait_ge(pick_in[b], r * (32 * (3 - b)) + 32 * (3 - b))
            pool.sem_inc(pool_turn, 1)

    @block.scalar
    def _(act):
        n = [0]

        def step(ins):
            n[0] += 1
            ins.then_inc(astep, 1)
            act.wait_ge(astep, n[0])

        act.wait_ge(cols_ready, 1)
        nc.scalar.activation(silc[:].rearrange("p k c -> p c k"), cols[:, 0:16].rearrange("p (c k) -> p c k", c=2),
                             ACT.Silu).then_inc(silc_ready, 1)
        for t in range(NT):
            act.wait_ge(x_loaded[t], 16)
            step(nc.scalar.activation(junk, x_in[:, t, :], ACT.Square, accum_out=stat[:, t:t + 1]))
        act.wait_ge(eps_ready, 1)
        step(nc.scalar.activation(stat[:, 8:8 + NT], stat[:, 0:NT], ACT.Ln, scale=1.0 / D, bias=stat[:, 60:61]))
        nc.scalar.activation(stat[:, 16:16 + NT], stat[:, 8:8 + NT], ACT.Exp, scale=-0.5).then_inc(rstd_ready, 1)
        for t in range(NT):
            act.wait_ge(xnT_done, t + 1)
            nc.scalar.activation(hTv[:, 0:4, t * P:(t + 1) * P],
                                 PS[:, 2 * (t % 2), :].rearrange("p (k s) -> p k s", k=4), ACT.Copy).then_inc(hraw_a, 1)
        def win_out(m):
            w, t = WIN_ORDER[m // NT], m % NT
            act.wait_ge(mm_done, m + 1)
            src = PS[:, m % 2, :]
            qs = float(QK) ** -0.5 if w == "dq" else 1.0
            heads = lambda v: v.rearrange("p (h d) -> p h d", h=H)
            if w == "mk":
                nc.scalar.activation(mk_tok[:, t], heads(src), ACT.Copy, scale=float(HD) ** -0.5).then_inc(mm_evac, 1)
            elif w == "mv":
                nc.scalar.activation(mv1[:, t, :, 0:HD], heads(src), ACT.Copy).then_inc(mm_evac, 1)
            elif w == "mo":
                nc.scalar.activation(sgo[:, t], src, ACT.Exp, scale=-1.0).then_inc(mm_evac, 1)
            elif w == "dv":
                nc.scalar.activation(dv_tok[:, t], heads(src), ACT.Copy).then_inc(mm_evac, 1)
                if t == 0:
                    act.wait_ge(mm_evac, m + 1)
                    act.dma_start(out["new_v"][0, 0].rearrange("t h d -> t (h d)"),
                                  PR[:, 7700:8212]).then_inc(outs, 16)
            else:
                rc = {"mq": 0, "dk": 1, "dq": 2}[w] * NT + t
                if rc >= 2:
                    act.wait_ge(win_T, NT + rc - 1)
                if w != "mq" and t > 0:
                    dst = xs[:, rc % 2].rearrange("p (g h j) -> p g h j", h=2, j=16)
                    s4 = src.rearrange("p (g h j) -> p g h j", h=2, j=16)
                    nc.scalar.activation(dst[:, :, 0, :], s4[:, :, 1, :], ACT.Copy, scale=qs)
                    nc.scalar.activation(dst[:, :, 1, :], s4[:, :, 0, :], ACT.Copy, scale=qs)
                nc.scalar.activation(xr[:, rc % 2], src, ACT.Copy, scale=qs).then_inc(mm_evac, 1)
                if w == "dk" and t == 0:
                    act.wait_ge(mm_evac, m + 1)
                    act.dma_start(out["new_k"][0, 0].rearrange("t h m d -> t (h m d)"), xr[:, rc % 2]).then_inc(outs, 16)
                    act.wait_ge(outs, 16)
            if w == "mk" and t == NT - 1:
                act.wait_ge(nabs_f, 1)
                step(nc.scalar.activation(ee, ee, ACT.Exp))
                nc.scalar.activation(ee, ee, ACT.Ln, bias=1.0).then_inc(softp, 1)
            if w == "mv" and t == 0:
                act.wait_ge(coef_args, 1)
                nc.scalar.activation(coef[:], coef[:], ACT.Exp).then_inc(coef_ready, 1)

        for m in range(ALONE * NT):
            win_out(m)
        for g, (d, t) in enumerate(MG):
            if g >= 1:
                win_out(ALONE * NT + 2 * g - 1)
            act.wait_ge(mb_done, g + 1)
            if g >= 2:
                act.wait_ge(sw_ready, g - 1)
            for h in range(H):
                ins = nc.scalar.activation(wexp[:, g % 2, h, :], PS[:, 5, h * P:(h + 1) * P], ACT.Exp,
                                           bias=gcol[:, 0, d, t, h:h + 1], scale=-1.0)
            ins.then_inc(w_ready, 1)
            win_out(ALONE * NT + 2 * g)
            if g < 2:
                act.wait_ge(newC_T, g + 1)
                nc.scalar.activation(newC[:, 4 * d:4 * d + 4, :], PS[:, 4, :].rearrange("p (h k) -> p h k", h=H),
                                     ACT.Copy).then_inc(newC_ready, 1)
            if g == 1:
                act.wait_ge(newC_ready, 2)
                act.dma_start(out["new_C"][0, 0].rearrange("d h v k -> v (d h) k"), newC).then_inc(outs, 16)
                act.wait_ge(ct_ready, 2)
                act.dma_start(out["new_n"][0, 0].rearrange("d h k -> k d h"), nout[:], allow_slow_non_contiguous=True).then_inc(outs, 16)
                act.dma_start(out["new_m"][0, 0].rearrange("d h -> h d"), newm[:], allow_slow_non_contiguous=True).then_inc(outs, 16)
        win_out(NT * len(WIN_ORDER) - 1)
        for n_ in (4, 5):
            act.dma_start(ada_b2[:, n_ % 2, :], a["b_ada"][0, n_ * 512:(n_ + 1) * 512].partition_broadcast(2)
                          ).then_inc(bias2_loaded[n_ % 2], 16)
        act.wait_ge(lam_args, 1)
        nc.scalar.activation(lam[:, 2:4], lam[:, 0:2], ACT.Exp).then_inc(lam_exp, 1)
        act.wait_ge(outs, 16 * 5)
        for u in range(NU + 4):
            if u < NU:
                h, j = UNITS[u]
                nk = CTX if j == 0 else LAT + PAST
                act.wait_ge(smax, 2 * u + 2)
                if u >= 2:
                    act.wait_ge(a_T, u - 1)
                for m in range(2):
                    nc.scalar.activation(pexp[:, u % 2, m, 0:nk], scores[:, m, 0:nk], ACT.Exp, bias=stat[:, 40 + m:41 + m],
                                         accum_out=stat[:, 42 + 2 * (u % 2) + m:43 + 2 * (u % 2) + m]).then_inc(pexp_done, 1)
            if u % NT == 1 and u > 1:
                hh = u // NT - 1
                act.wait_ge(pv_done, hh + 1)
                nc.scalar.activation(osq[:, CTX:T], PS[:, 6, :], ACT.Square)
                act.wait_ge(pvc_done, hh + 1)
                nc.scalar.activation(octx, PS[:, 3, P:2 * P], ACT.Copy)
                nc.scalar.activation(osq[:, 0:CTX], PS[:, 3, P:2 * P], ACT.Square).then_inc(osq_ready, 1)
            if u % NT == 2 and u > 2:
                hh = u // NT - 1
                act.wait_ge(ossc_done, hh + 1)
                nc.scalar.activation(osq[:, 0:CTX], PS[:, 4, P:2 * P], ACT.Copy).then_inc(ossc_read, 1)
            if 1 <= u <= NU:
                h, j = UNITS[u - 1]
                act.wait_ge(a_T, u)
                if j == 0:
                    if h >= 2:
                        act.wait_ge(pv_done, h - 1)
                    nc.scalar.activation(aTc[:, h % 2, :], PS[:, 3, 0:P], ACT.Copy).then_inc(aT_ready, 1)
                else:
                    nc.scalar.activation(aT[:, h % 2, :, (j - 1) * P:j * P], aT_ps.rearrange("p (k q) -> p k q", k=5),
                                         ACT.Copy).then_inc(aT_ready, 1)
            if u % NT == 2 and u > 2:
                hh = u // NT - 1
                act.wait_ge(oss_done, hh + 1)
                nc.scalar.activation(osq[:, CTX:T], PS[:, 7, :], ACT.Ln, scale=1.0 / HD, bias=stat[:, 60:61])
                act.wait_ge(ossc_read, hh + 1)
                step(nc.scalar.activation(osq[:, 0:CTX], osq[:, 0:CTX], ACT.Ln, scale=1.0 / HD, bias=stat[:, 60:61]))
                nc.scalar.activation(osq, osq, ACT.Exp, scale=-0.5).then_inc(orstd, 1)
            if u == NT:
                act.wait_ge(hn_ss, NT)
                r20 = stat[:, 20:20 + 4 * NT]
                step(nc.scalar.activation(r20, r20, ACT.Ln, scale=1.0 / HD, bias=stat[:, 60:61]))
                nc.scalar.activation(r20, r20, ACT.Exp, scale=-0.5).then_inc(hn_rstd, 1)
            if u in MIX_STEPS:
                t = MIX_STEPS.index(u)
                act.wait_ge(mix_T, t + 1)
                src = mix_bank(t)
                for hh in range(H):
                    ins = nc.scalar.activation(hTv[:, hh, t * P:(t + 1) * P], src[:, hh * P:(hh + 1) * P], ACT.Copy,
                                               scale=cols[:, 24 + hh:25 + hh])
                ins.then_inc(mix_ready, 1)
            for n_ in range(4, 12):
                if u == ada_step(n_) + 2:
                    act.wait_ge(ada_row, n_ + 1)
                    act.dma_start(scratch["mod"][:, (n_ - 4) * 512:(n_ - 3) * 512], ada_b2[:, n_ % 2, :]).then_inc(row_stored, 16)
                if u == ada_step(n_) + 3 and n_ + 2 < 12:
                    act.wait_ge(row_stored, 16 * (n_ - 3))
                    act.dma_start(ada_b2[:, n_ % 2, :], a["b_ada"][0, (n_ + 2) * 512:(n_ + 3) * 512].partition_broadcast(2)
                                  ).then_inc(bias2_loaded[n_ % 2], 16)
        for t in range(NT + 2):
            if 1 <= t <= NT:
                tt = t - 1
                act.wait_ge(h2_T, tt + 1)
                for k2 in range(2):
                    ins = nc.scalar.activation(hTv[:, 4 * k2:4 * k2 + 4, tt * P:(tt + 1) * P],
                                               PS[:, 4 + k2, :].rearrange("p (k s) -> p k s", k=4), ACT.Copy)
                ins.then_inc(h2T_ready, 1)
            if t >= 2:
                tt = t - 2
                act.wait_ge(route_arg, tt + 1)
                nc.scalar.activation(rt[:, 1, tt, :], rt[:, 1, tt, :], ACT.Exp, accum_out=rs[:, 7, tt:tt + 1])
                nc.scalar.activation(rs[:, 2, tt:tt + 1], rs[:, 2, tt:tt + 1], ACT.Exp).then_inc(route_exp, 1)
            if 1 <= t <= NT:
                act.wait_ge(logT, t)
                if t >= 2:
                    act.wait_ge(route_done, t - 1)
                nc.scalar.activation(lgT[:], PS[0:20, 6, 0:P], ACT.Identity, bias=broute[:]).then_inc(logT_read, 1)
            if t < NT:
                act.wait_ge(x1_ready, 2 * (t + 1))
                step(nc.scalar.activation(junkn, x1[:, t, :], ACT.Square, accum_out=stat[:, t:t + 1]))
                step(nc.scalar.activation(stat[:, 8 + t:9 + t], stat[:, t:t + 1], ACT.Ln, scale=1.0 / D, bias=stat[:, 60:61]))
                nc.scalar.activation(stat[:, 16 + t:17 + t], stat[:, 8 + t:9 + t], ACT.Exp, scale=-0.5).then_inc(n2_rstd, 1)
                act.wait_ge(h2_ready, t + 1)
                act.dma_start(scratch["h2"][t * P:(t + 1) * P, :], h2[:, t % 2, :]).then_inc(h2_stored[t % 2], 16)
        act.wait_ge(rounds_ready, 1)
        n_rounds = act.value_load(rnd[0:1, 0:1], min_val=1, max_val=ROUNDS)
        for b in range(2):
            act.sem_inc(yo_ready[b], 1)
            act.sem_inc(yo_stored[b], 16)
        act.sem_inc(fin_rstd, NT)
        act.sem_inc(x2_ready, NT)
        with act.Fori(0, n_rounds) as r:
            with act.Fori(0, PAIRS) as q:
                it = r * PAIRS + q
                for b in range(2):
                    act.wait_ge(gu_done[b], it + 2)
                    nc.scalar.activation(sil[:, b, :], PS[:, 4 + b, 0:EH], ACT.Silu).then_inc(sil_ready[b], 1)
                for b in range(2):
                    act.wait_ge(dn_done[b], it + 2)
                    act.wait_ge(yo_stored[b], 16 * it + 16)
                    nc.scalar.activation(yo[:, b, 0:512], PS[:, 2 * b, :], ACT.Copy)
                    nc.scalar.activation(yo[:, b, 512:D], PS[:, 2 * b + 1, :], ACT.Copy).then_inc(yo_ready[b], 1)
                    act.wait_ge(yo_ready[b], it + 2)
                    act.dma_start(scratch["y"][bass.ds(q * 256 + b * P, P), :], yo[:, b, :]).then_inc(yo_stored[b], 16)
            for t in range(NT + 1):
                if t < NT:
                    uses = 3 - t % 2
                    act.wait_ge(pick_in[t % 2], r * (32 * uses) + 32 * (t // 2 + 1))
                    if t == 0:
                        act.wait_ge(pick_w, r + 1)
                    y0 = ypick[:, t % 2, 0]
                    nc.scalar.activation(y0, y0, ACT.Copy, scale=rs[:, 20, t:t + 1]).then_inc(y_scaled, 1)
                if t >= 1:
                    act.wait_ge(y_sum, r * NT + (t + 2))
                    nc.scalar.activation(junkn, x1[:, t - 1, :], ACT.Square, accum_out=stat[:, t - 1:t]).then_inc(x2_ready, 1)
                    act.wait_ge(x2_ready, r * NT + (NT + t))
                    nc.scalar.activation(stat[:, 7 + t:8 + t], stat[:, t - 1:t], ACT.Ln, scale=1.0 / D,
                                         bias=stat[:, 60:61]).then_inc(fin_ln, 1)
                    act.wait_ge(fin_ln, r * NT + t)
                    nc.scalar.activation(stat[:, 15 + t:16 + t], stat[:, 7 + t:8 + t], ACT.Exp, scale=-0.5).then_inc(fin_rstd, 1)

    @block.vector
    def _(dve):
        n = [0]
        V = nc.vector

        def step(ins):
            n[0] += 1
            ins.then_inc(dstep, 1)
            dve.wait_ge(dstep, n[0])

        V.memset(stat[:, 60:61], EPS).then_inc(eps_ready, 1)
        dve.wait_ge(cols_T, 1)
        V.tensor_copy(cols[:, 0:28], PS[:, 7, 0:28])
        V.tensor_scalar(cols[:, 28:32], PS[:, 7, 28:32], 1.0 - LAM_INIT, None, ALU.mult)
        V.tensor_copy(cols[:, 32:40], PS[:, 7, 32:40]).then_inc(cols_ready, 1)
        dve.wait_ge(rstd_ready, 1)
        for t in range(NT):
            if t >= 2:
                dve.wait_ge(xnT_done, t - 1)
            V.tensor_scalar(xn[:, t % 2, :], x_in[:, t, :], stat[:, 16 + t:17 + t], None, ALU.mult).then_inc(xn_ready, 1)
            if t >= 1:
                dve.wait_ge(xnT_done, t)
                V.tensor_copy(hTv[:, 4:8, (t - 1) * P:t * P],
                              PS[:, 2 * ((t - 1) % 2) + 1, :].rearrange("p (k s) -> p k s", k=4)).then_inc(hraw_v, 1)
        dve.wait_ge(xnT_done, NT)
        V.tensor_copy(hTv[:, 4:8, (NT - 1) * P:NT * P],
                      PS[:, 2 * ((NT - 1) % 2) + 1, :].rearrange("p (k s) -> p k s", k=4)).then_inc(hraw_v, 1)
        dve.wait_ge(small_loaded, 16 * SMALL)
        V.tensor_copy(identb[:], ident[:])
        V.tensor_copy(masksb[:], masks[:])
        V.tensor_copy(tokid[:], misc[:, 32:37])
        V.memset(gzero, 0.0)

        def ada_rows(n_):
            dve.wait_ge(ada_done, n_ + 1)
            if n_ < 4:
                dve.wait_ge(bias_loaded[n_ % 2], 16 * (n_ // 2 + 1))
            else:
                dve.wait_ge(bias2_loaded[n_ % 2], 16 * (n_ // 2 - 1))
            row = (ada_b1 if n_ < 4 else ada_b2)[:, n_ % 2, :]
            last = V.tensor_tensor(row, PS[0:2, 4 + n_ % 2 if n_ < 4 else 5, :], row, ALU.add)
            if n_ in (8, 9):
                step(last)
                last = V.scalar_tensor_tensor(row, row, 1.0, ada_g[:, (n_ - 8) * 512:(n_ - 7) * 512], ALU.add, ALU.mult)
            last.then_inc(ada_row, 1)

        for n_ in range(4):
            ada_rows(n_)
        dve.wait_ge(adacol_T, 4)
        V.tensor_copy(modc[:, 0:8, :], PS[:, 6, 0:16].rearrange("p (k c) -> p k c", c=2))
        step(V.scalar_tensor_tensor(modc[:, 8:16, :], PS[:, 6, 16:32].rearrange("p (k c) -> p k c", c=2), 1.0,
                                    cols[:, 16:24].unsqueeze(2).broadcast_to([P, KD, 2]), ALU.add, ALU.mult))
        dve.wait_ge(hraw_a, NT)
        dve.wait_ge(hraw_v, NT)
        for k in range(KD):
            for c, (lo, hi) in enumerate(((0, CTX), (CTX, T))):
                last = V.tensor_scalar(hTv[:, k, lo:hi], hTv[:, k, lo:hi], modc[:, 8 + k, c:c + 1], modc[:, k, c:c + 1],
                                       ALU.mult, ALU.add)
            last.then_inc(h_ready, 1)
        V.memset(mv1[:, :, :, HD:HD + 1], 1.0)
        dve.wait_ge(gate_done, 1)
        V.tensor_scalar(grow, PS[0:16, 6:8, :].rearrange("p b n -> p (b n)")[:, 0:T], bgate[:], None, ALU.add
                        ).then_inc(gate_rows, 1)
        dve.wait_ge(gate_split, 64)
        step(V.scalar_tensor_tensor(ee, gf, -1.0, gf, ALU.mult, ALU.min))
        dve.sem_inc(nabs_f, 1)

        DST = {"mk": mkT, "mq": mqT, "dk": dkT, "dq": dqT}

        def win_evac(m):
            w, t = WIN_ORDER[m // NT], m % NT
            if w not in DST:
                return
            tn = T_NO[m]
            dve.wait_ge(win_T, tn + 1)
            V.tensor_copy(DST[w][:, :, t * P:(t + 1) * P], PS[:, 2 + tn % 2, :].rearrange("p (h s) -> p h s", h=H)
                          ).then_inc(win_Tevac, 1)

        def win_finish(m):
            w, t = WIN_ORDER[m // NT], m % NT
            if w in ("dk", "dq") and t > 0:
                dve.wait_ge(mm_evac, m + 1)
                rc = T_NO[m] - NT
                dve.wait_ge(win_T, NT + rc - 1)
                b = rc % 2
                g = lambda v: v.rearrange("p (g j) -> p g j", j=QK)
                V.tensor_tensor(g(rr[:, b]), g(xr[:, b]), rope[:, 0, t - 1, :].unsqueeze(1).broadcast_to([P, 8, QK]), ALU.mult)
                step(V.tensor_tensor(g(xs[:, b]), g(xs[:, b]), rope[:, 1, t - 1, :].unsqueeze(1).broadcast_to([P, 8, QK]), ALU.mult))
                V.tensor_tensor(rr[:, b], rr[:, b], xs[:, b], ALU.add).then_inc(roped, 1)
            if w == "mo":
                dve.wait_ge(mm_evac, m + 1)
                step(V.tensor_scalar(sgo[:, t], sgo[:, t], 1.0, None, ALU.add))
                step(V.reciprocal(sgo[:, t], sgo[:, t]))

        for m in range(2 * NT):
            w, t = WIN_ORDER[m // NT], m % NT
            win_evac(m)
            if w == "mk" and t == NT - 1:
                dve.wait_ge(softp, 1)
                step(V.scalar_tensor_tensor(gf, gf, 0.0, ee, ALU.min, ALU.subtract))
                spans = [(0, 0, CTX), (0, CTX, T), (1, 0, CTX), (1, CTX, T)]

                def along(v, d, lo, hi):
                    return v[:, d, lo:hi] if d == 0 else v[:, d, lo:hi][:, ::-1]

                for d, lo, hi in spans:
                    last = V.tensor_tensor_scan(along(ee, d, lo, hi), along(gf, d, lo, hi), gzero[:, 0:hi - lo],
                                                0.0, ALU.add, ALU.add)
                step(last)
                step(V.tensor_tensor(gi, gi, ee, ALU.subtract))
                for d, lo, hi in spans:
                    last = V.tensor_tensor_scan(along(gf, d, lo, hi), along(gi, d, lo, hi), gzero[:, 0:hi - lo],
                                                0.0 if lo == 0 else sm_in[:, d:d + 1], ALU.max, ALU.add)
                step(last)
                step(V.tensor_tensor(ee, ee, gf, ALU.add))
                V.tensor_copy(newm[:, 0:1], ee[:, 0, CTX - 1:CTX])
                step(V.tensor_copy(newm[:, 1:2], ee[:, 1, 0:1]))
                for d, e in ((0, P - 1), (1, 0)):
                    ends = gf[:, d, :].rearrange("p (t s) -> p t s", s=P)[:, :, e:e + 1].broadcast_to([H, NT, H])
                    last = V.tensor_tensor(mendd[:, d], ends, eye4[:], ALU.mult)
                last.then_inc(mendd_ready, 1)
                dve.wait_ge(mend_bc, 1)
                V.tensor_copy(gcol[:].rearrange("p a d t h -> p (a d t h)"), PS[:, 6, 0:120])
                dve.wait_ge(mend_bc, 1)
                step(V.tensor_copy(mend[:].rearrange("p d t h -> p (d t h)"), PS[:, 7, 0:40]))
                V.memset(mprev[:, :, 0, :], 0.0)
                V.tensor_copy(mprev[:, 0, 2:5, :], mend[:, 0, 1:4, :])
                V.tensor_copy(mprev[:, 1, 1:4, :], mend[:, 1, 2:5, :])
                V.tensor_copy(mprev[:, 0, 1, :], m0b[:, 0, :])
                step(V.tensor_copy(mprev[:, 1, 4, :], m0b[:, 1, :]))
                V.tensor_tensor(coef[:, 0], gcol[:, 0], mend[:], ALU.subtract)
                V.tensor_tensor(coef[:, 1], mprev[:], gcol[:, 1], ALU.subtract)
                V.tensor_tensor(coef[:, 2], mprev[:], mend[:], ALU.subtract)
                step(V.tensor_scalar(coef[:, 3], gcol[:, 2], -1.0, None, ALU.mult))
                dve.sem_inc(coef_args, 1)
        step(V.tensor_tensor(lamb[:, 0::2, :], lamb[:, 0::2, :], lamb[:, 1::2, :], ALU.mult))
        V.tensor_reduce(lam[:, 0:2], lamb[:, 0::2, :], AX.X, ALU.add).then_inc(lam_args, 1)
        dve.wait_ge(state_T, 1)
        for d in range(2):
            V.tensor_copy(CT[:, d, 0, :, 0:HD], PS[:, 6 + d, :].rearrange("p (h v) -> p h v", h=H))
            last = V.tensor_copy(CT[:, d, 0, :, HD:HD + 1], cols[:, 32 + 4 * d:36 + 4 * d].unsqueeze(2))
        last.then_inc(ct0_ready, 1)
        dve.wait_ge(ck_T, 1)
        V.tensor_copy(ckT, PS[:, 4, :].rearrange("p (h s) -> p h s", h=H)).then_inc(ck_ready, 1)

        two = lambda v: v.rearrange("p (b h) v -> p b h v", b=2)
        bank2 = PS[:, 6:8, 0:258].rearrange("p b (h v) -> p b h v", h=2)
        seen = set()
        for g, (d, t) in enumerate(MG):
            unit_a, unit_b0 = ALONE * NT + 2 * g, ALONE * NT + 2 * g - 1
            if g >= 1:
                win_finish(unit_b0)
            dve.wait_ge(w_ready, g + 1)
            dve.wait_ge(st_done, g + 1)
            if g >= 2:
                dve.wait_ge(num_done, g - 1)
            V.tensor_tensor(sw[:, g % 2], PS[:, 4, :].rearrange("p (h t) -> p h t", h=H), wexp[:, g % 2],
                            ALU.mult).then_inc(sw_ready, 1)
            if g < NUPD:
                i = (g // 2) - 1
                dve.wait_ge(upd_done, g + 1)
                if i < 0:
                    V.tensor_copy(two(CT[:, d, 1]), bank2)
                    V.tensor_copy(nout[:, d, :].rearrange("p (b h) -> p b h", b=2), bank2[:, :, :, HD]).then_inc(ct_ready, 1)
                else:
                    dec = coef[:, 2, d, t, :].unsqueeze(2).broadcast_to([P, H, HD + 1])
                    src, dst = CT[:, d, i % 2], CT[:, d, (i + 1) % 2]
                    if i == 0:
                        dve.wait_ge(newC_T, g - 1)
                    else:
                        dve.wait_ge(int_done, g - 3)
                    step(V.tensor_tensor(dst, src, dec, ALU.mult))
                    V.tensor_tensor(two(dst), two(dst), bank2, ALU.add).then_inc(ct_ready, 1)
            if g >= 1:
                win_evac(unit_b0)
            win_finish(unit_a)
            if t > 0:
                dve.wait_ge(int_done, g - 1)
                ws = coef[:, 1, d, t, :].rearrange("p (b h) -> p b h", b=2).unsqueeze(3).broadcast_to([P, 2, 2, HD + 1])
                step(V.tensor_tensor(two(num), bank2, ws, ALU.mult))
                dve.sem_inc(int_read, 1)
            dve.wait_ge(num_done, g + 1)
            if t == 0:
                step(V.tensor_copy(two(num), bank2))
            else:
                step(V.tensor_tensor(two(num), two(num), bank2, ALU.add))
            dve.sem_inc(num_read, 1)
            den = stat[:, 56:60]
            step(V.scalar_tensor_tensor(den, num[:, :, HD], -1.0, num[:, :, HD], ALU.mult, ALU.max))
            step(V.tensor_tensor(den, den, coef[:, 3, d, t, :], ALU.max))
            step(V.reciprocal(den, den))
            rb_ = den.unsqueeze(2).broadcast_to([P, H, HD])
            if t not in seen:
                seen.add(t)
                step(V.tensor_tensor(hm[:, t], num[:, :, 0:HD], rb_, ALU.mult))
            else:
                step(V.tensor_tensor(num[:, :, 0:HD], num[:, :, 0:HD], rb_, ALU.mult))
                step(V.tensor_tensor(hm[:, t], hm[:, t], num[:, :, 0:HD], ALU.add))
            win_evac(unit_a)
        dve.sem_inc(hm_ready, 1)
        dve.wait_ge(lam_exp, 1)
        step(V.scalar_tensor_tensor(lam[:, 4:5], lam[:, 3:4], -LAM_INIT, lam[:, 2:3], ALU.add, ALU.subtract))
        for u in range(NU + 4):
            for n_ in range(4, 12):
                if u == ada_step(n_) + 1:
                    ada_rows(n_)
            if u < NU:
                h, j = UNITS[u]
                for m in range(2):
                    dve.wait_ge(sc_done, 2 * u + 2)
                    if u >= 1:
                        dve.wait_ge(pexp_done, 2 * (u - 1) + m + 1)
                    V.tensor_reduce(stat[:, 40 + m:41 + m], scores[:, m, 0:CTX if j == 0 else LAT + PAST], AX.X, ALU.max,
                                    negate=True).then_inc(smax, 1)
            if u == 1:
                win_finish(NT * len(WIN_ORDER) - 1)
                dve.sem_inc(sg_ready, 1)
            if u < NT:
                dve.wait_ge(hn_sq, u + 1)
                V.tensor_reduce(stat[:, 20 + 4 * u:24 + 4 * u], hsq[:, u], AX.X, ALU.add).then_inc(hn_ss, 1)
            if u < NU:
                nk = CTX if j == 0 else LAT + PAST
                b = u % 2
                l0, l1 = stat[:, 42 + 2 * b:43 + 2 * b], stat[:, 43 + 2 * b:44 + 2 * b]
                dve.wait_ge(pexp_done, 2 * u + 1)
                step(V.reciprocal(stat[:, 46:47], l0))
                V.tensor_scalar(pexp[:, b, 0, 0:nk], pexp[:, b, 0, 0:nk], stat[:, 46:47], None, ALU.mult)
                dve.wait_ge(pexp_done, 2 * u + 2)
                step(V.reciprocal(stat[:, 61:62], l1))
                step(V.tensor_tensor(stat[:, 62:63], lam[:, 4:5], stat[:, 61:62], ALU.mult))
                V.scalar_tensor_tensor(pexp[:, b, 0, 0:nk], pexp[:, b, 1, 0:nk], stat[:, 62:63], pexp[:, b, 0, 0:nk],
                                       ALU.mult, ALU.add).then_inc(a_ready, 1)
            if u % NT == 3 and u > 3:
                hh = u // NT - 1
                dve.wait_ge(orstd, hh + 1)
                gain = cols[:, 28 + hh:29 + hh]
                V.scalar_tensor_tensor(hTv[:, 4 + hh, CTX:T], PS[:, 6, :], gain, osq[:, CTX:T], ALU.mult, ALU.mult)
                V.scalar_tensor_tensor(hTv[:, 4 + hh, 0:CTX], octx, gain, osq[:, 0:CTX], ALU.mult, ALU.mult
                                       ).then_inc(omix, 1)
        dve.wait_ge(g1_loaded, 32)
        prio = misc[:, 16:20]
        expert = misc[:, 0:NE].unsqueeze(1).broadcast_to([P, 2, NE])

        def first_max(src, mx, val, vmax, hot):
            step(V.tensor_reduce(mx, src, AX.X, ALU.max))
            step(V.scalar_tensor_tensor(val, src, mx, prio, ALU.is_equal, ALU.mult))
            step(V.tensor_reduce(vmax, val, AX.X, ALU.max))
            step(V.tensor_scalar(hot, val, vmax, None, ALU.is_equal))

        def route(t):
            R = lambda i: rs[:, i, t:t + 1]
            Q = lambda i: rt[:, i, t, :]
            v16 = lambda i: r16[:, i, t].rearrange("p (g j) -> p g j", g=NG)
            dve.wait_ge(route_done, t + 1)
            step(V.tensor_copy(lgt[:, t], PS[:, 6, 128:148]))
            lg = lgt[:, t, 0:4]
            first_max(lg, R(0), Q(3), R(1), Q(0))
            V.tensor_scalar(Q(1), lg, R(0), None, ALU.subtract)
            gh = Q(0).unsqueeze(2).broadcast_to([P, NG, EG])
            step(V.tensor_tensor(v16(2), lgt[:, t, 4:20].rearrange("p (g j) -> p g j", g=NG), gh, ALU.mult))
            step(V.tensor_reduce(Q(4), v16(2).rearrange("p g j -> p j g"), AX.X, ALU.add))
            first_max(Q(4), R(3), Q(6), R(4), Q(7))
            step(V.scalar_tensor_tensor(Q(8), Q(7), -BIG, Q(4), ALU.mult, ALU.add))
            first_max(Q(8), R(5), Q(10), R(6), Q(11))
            V.tensor_tensor(R(2), R(5), R(3), ALU.subtract).then_inc(route_arg, 1)
            V.tensor_tensor(v16(0), gh, Q(7).unsqueeze(1).broadcast_to([P, NG, EG]), ALU.mult)
            step(V.tensor_tensor(v16(1), gh, Q(11).unsqueeze(1).broadcast_to([P, NG, EG]), ALU.mult))
            V.tensor_tensor(ohb[:, t], r16[:, 0, t], r16[:, 1, t], ALU.add).then_inc(oh_ready, 1)

        def place(t):
            R = lambda i: rs[:, i, t:t + 1]
            picks, prod = r16[:, 0:2, t, :], r16[:, 2:4, t, :]
            step(V.tensor_tensor(prod, expert, picks, ALU.mult))
            V.tensor_reduce(rs[:, 14:16, t], prod, AX.X, ALU.add)
            dve.wait_ge(route_exp, t + 1)
            step(V.scalar_tensor_tensor(R(8), R(2), 1.0, R(7), ALU.add, ALU.mult))
            step(V.reciprocal(R(9), R(8)))
            step(V.tensor_tensor(R(10), R(9), R(2), ALU.mult))
            dve.wait_ge(rank_done, t + 1)
            rank = PS[:, 7, NE * t:NE * t + NE].unsqueeze(1).broadcast_to([P, 2, NE])
            step(V.tensor_tensor(prod, rank, picks, ALU.mult))
            step(V.tensor_reduce(rs[:, 12:14, t], prod, AX.X, ALU.add))
            r2, e2, b2, s2 = (rs[:, i:i + 2, t] for i in (12, 14, 16, 18))
            V.scalar_tensor_tensor(s2, e2, float(P), r2, ALU.mult, ALU.add)
            step(V.tensor_scalar(b2, r2, float(P), None, ALU.is_ge))
            for k in range(2, ROUNDS):
                step(V.scalar_tensor_tensor(b2, r2, float(k * P), b2, ALU.is_ge, ALU.add))
            V.scalar_tensor_tensor(slot[:, 0:2, t], r2, float(NE), e2, ALU.mult, ALU.add)
            step(V.scalar_tensor_tensor(slot[:, 2:4, t], b2, float(-P), s2, ALU.mult, ALU.add))
            dve.sem_inc(slots_ready, 1)

        for t in range(NT + 2):
            for q in range(2):
                if t < NT:
                    c = min(t, 1)
                    i = 2 * t + q
                    if q == 0:
                        dve.wait_ge(x_loaded[t], 32)
                    dve.wait_ge(o_done, i + 1)
                    step(V.tensor_tensor(mixg[:, q], PS[:, i % 4, :], g1b[:, c, q * 512:(q + 1) * 512], ALU.mult))
                    V.tensor_tensor(x1[:, t, q * 512:(q + 1) * 512], x1[:, t, q * 512:(q + 1) * 512], mixg[:, q],
                                    ALU.add).then_inc(x1_ready, 1)
                if q == 0 and t >= 2:
                    route(t - 2)
            if t < NT:
                dve.wait_ge(n2_rstd, t + 1)
                if t == 0:
                    dve.wait_ge(mod_loaded, 64)
                if t >= 2:
                    dve.wait_ge(h2_stored[t % 2], 16 * (t // 2))
                    dve.wait_ge(h2_T, t - 1)
                step(V.scalar_tensor_tensor(h2[:, t % 2], x1[:, t], stat[:, 16 + t:17 + t], mod2[:, 1, c], ALU.mult, ALU.mult))
                V.tensor_tensor(h2[:, t % 2], h2[:, t % 2], mod2[:, 0, c], ALU.add).then_inc(h2_ready, 1)
            if t >= 2:
                place(t - 2)
        step(V.tensor_reduce(cnt[:, 0:1], PS[:, 7, 80:96], AX.X, ALU.max))
        step(V.tensor_scalar(cnt[:, 1:2], cnt[:, 0:1], float(P), 1.0, ALU.is_gt, ALU.add))
        for k in range(2, ROUNDS):
            step(V.scalar_tensor_tensor(cnt[:, 1:2], cnt[:, 0:1], float(k * P), cnt[:, 1:2], ALU.is_gt, ALU.add))
        step(V.tensor_copy(rnd[:], cnt[:, 1:2]))
        dve.sem_inc(rounds_ready, 1)
        dve.wait_ge(g2_loaded, 32)
        n_rounds = dve.value_load(rnd[0:1, 0:1], min_val=1, max_val=ROUNDS)
        for b in range(2):
            dve.sem_inc(hid_ready[b], 1)
            dve.sem_inc(hidT_ready[b], 1)
        dve.sem_inc(y_sum, 2)
        base = n[0]
        PER_ROUND = 2 + 2 * NT
        with dve.Fori(0, n_rounds) as r:
            with dve.Fori(0, PAIRS) as q:
                it = r * PAIRS + q
                for b in range(2):
                    dve.wait_ge(xg_T[b], it + 2)
                    dve.wait_ge(gu_done[b], it + 1)
                    for k2 in range(2):
                        last = V.tensor_copy(xgT[:, b, 4 * k2:4 * k2 + 4, :],
                                             PS[:, 2 * b + k2, :].rearrange("p (k s) -> p k s", k=4))
                    last.then_inc(xgT_ready[b], 1)
                for b in range(2):
                    dve.wait_ge(sil_ready[b], it + 1)
                    V.tensor_tensor(hid[:, b], sil[:, b], PS[:, 4 + b, EH:2 * EH], ALU.mult).then_inc(hid_ready[b], 1)
                    dve.wait_ge(hid_T[b], it + 1)
                    dve.wait_ge(dn_done[b], it + 1)
                    V.tensor_copy(hidT[:, b], PS[:, 6, 256 * b:256 * b + 256].rearrange("p (k s) -> p k s", k=2)
                                  ).then_inc(hidT_ready[b], 1)
            n[0] = 0

            def rstep(ins):
                n[0] += 1
                ins.then_inc(dstep, 1)
                dve.wait_ge(dstep, r * PER_ROUND + (base + n[0]))

            rstep(V.scalar_tensor_tensor(rs[:, 20:22], rs[:, 16:18], 0.0, rs[:, 9:11], ALU.is_equal, ALU.mult))
            dve.sem_inc(pick_w, 1)
            rstep(V.tensor_scalar(rs[:, 16:18], rs[:, 16:18], -1.0, None, ALU.add))
            for t in range(NT):
                c = min(t, 1)
                uses = 3 - t % 2
                dve.wait_ge(pick_in[t % 2], r * (32 * uses) + 32 * (t // 2 + 1))
                dve.wait_ge(y_scaled, r * NT + (t + 1))
                y0, y1 = ypick[:, t % 2, 0], ypick[:, t % 2, 1]
                rstep(V.scalar_tensor_tensor(y0, y1, rs[:, 21, t:t + 1], y0, ALU.mult, ALU.add))
                rstep(V.tensor_tensor(y0, y0, g2b[:, c], ALU.mult))
                dve.wait_ge(x2_ready, r * NT + (t + 1))
                V.tensor_tensor(x1[:, t], x1[:, t], y0, ALU.add).then_inc(y_sum, 1)
            assert n[0] == PER_ROUND
            dve.wait_ge(y_sum, r * NT + (NT + 2))
        dve.wait_ge(fnorm_loaded, 16)
        for t in range(NT):
            dve.wait_ge(fin_rstd, n_rounds * NT + (t + 1))
            V.scalar_tensor_tensor(x1[:, t], x1[:, t], stat[:, 16 + t:17 + t], fnorm[:], ALU.mult, ALU.mult
                                   ).then_inc(fin_ready, 1)

    @block.tensor
    def _(pe):
        mm = nc.tensor.matmul
        tr = nc.tensor.transpose

        pe.wait_ge(vec_loaded, 16 * 7)
        tr(PS[:, 7, 0:40], vrows[:], ident[0:40, 0:40]).then_inc(cols_T, 1)

        def xn_T(t):
            pe.wait_ge(xn_ready, t + 1)
            if t >= 2:
                pe.wait_ge(hraw_a, t - 1)
                pe.wait_ge(hraw_v, t - 1)
            for k in range(KD):
                last = tr(PS[:, 2 * (t % 2) + k // 4, (k % 4) * P:(k % 4 + 1) * P], xn[:, t % 2, k * P:(k + 1) * P], ident[:])
            last.then_inc(xnT_done, 1)

        def halves(ci, hf):
            pe.wait_ge(half_in[2 * (ci % 2) + hf], 16 * (ci // 2 + 1))

        def ada(n_, ci):
            if n_ >= 2:
                pe.wait_ge(ada_row, n_ - 1)
            for k in range(KD):
                if k % 4 == 0:
                    halves(ci, k // 4)
                last = mm(PS[0:2, 4 + n_ % 2, :], silc[:, k, :], ring[:, ci % 2, k, :], start=(k == 0), stop=(k == KD - 1))
            last.then_inc(ada_done, 1)

        def ada_cols(n_):
            pe.wait_ge(ada_row, n_ + 1)
            for j in range(4):
                last = tr(PS[:, 6, 2 * (4 * n_ + j):2 * (4 * n_ + j) + 2], ada_b1[:, n_ % 2, j * P:(j + 1) * P], ident[0:2, 0:2])
            last.then_inc(adacol_T, 1)

        pe.wait_ge(silc_ready, 1)
        for n_ in range(4):
            ada(n_, ADA1 + n_)
            for t in range(NT):
                if 3 * n_ <= t < 3 * n_ + 3:
                    xn_T(t)
            if n_ >= 1:
                ada_cols(n_ - 1)
        ada_cols(3)
        pe.wait_ge(small_loaded, 16 * SMALL)
        for k in range(KD):
            pe.wait_ge(h_ready, k + 1)
            for bank, lo, hi in ((6, 0, 512), (7, 512, T)):
                last = mm(PS[0:16, bank, 0:hi - lo], wgate[:, k, :], hTv[:, k, lo:hi], start=(k == 0), stop=(k == KD - 1))
        last.then_inc(gate_done, 1)

        def proj(m, hf):
            c, t = m // NT, m % NT
            ci = WIN0 + c
            if m >= 2 and hf == 0:
                pe.wait_ge(mm_evac, m - 1)
            if t == 0:
                halves(ci, hf)
            for k in range(4 * hf, 4 * hf + 4):
                last = mm(PS[:, m % 2, :], hTv[:, k, t * P:(t + 1) * P], ring[:, ci % 2, k, :],
                          start=(k == 0), stop=(k == KD - 1))
            if hf == 1:
                last.then_inc(mm_done, 1)

        def heads_T(m):
            if m not in T_NO:
                return
            w, t, tn = WIN_ORDER[m // NT], m % NT, T_NO[m]
            if w in ("dk", "dq") and t > 0:
                pe.wait_ge(roped, tn - (11 if w == "dk" else 12) + 1)
                src = rr[:, (tn - NT) % 2]
            elif w == "mk":
                pe.wait_ge(mm_evac, m + 1)
                src = mk_tok[:, t].rearrange("p h d -> p (h d)")
            else:
                pe.wait_ge(mm_evac, m + 1)
                src = xr[:, (tn - NT) % 2]
            if tn >= 2:
                pe.wait_ge(win_Tevac, tn - 1)
            for h in range(H):
                last = tr(PS[:, 2 + tn % 2, h * P:(h + 1) * P], src[:, h * P:(h + 1) * P], ident[:])
            last.then_inc(win_T, 1)

        for m in range(ALONE * NT):
            w, t = WIN_ORDER[m // NT], m % NT
            proj(m, 0)
            proj(m, 1)
            if m >= 1:
                heads_T(m - 1)
            if w == "mq" and t == 2:
                pe.wait_ge(mendd_ready, 1)
                for i, v in enumerate((gi, gf, ee)):
                    for d in range(2):
                        for tt in range(NT):
                            o = ((i * 2 + d) * NT + tt) * H
                            last = tr(PS[:, 6, o:o + H], v[:, d, tt * P:(tt + 1) * P], ident[0:H, 0:H])
                mm(PS[:, 7, 0:40], ones4[:], mendd[:].rearrange("p d t h -> p (d t h)"), start=True, stop=True).then_inc(mend_bc, 1)
            if w == "mv" and t == 1:
                pe.wait_ge(coef_args, 1)
                for e in range(8):
                    last = tr(PS[:, 6 + e // 4, (e % 4) * P:(e % 4 + 1) * P], sC[:, e, :], ident[:])
                last.then_inc(state_T, 1)
            if w == "mv" and t == 3:
                pe.wait_ge(cache_loaded, 32)
                for h in range(H):
                    last = tr(PS[:, 4, h * P:(h + 1) * P], kc[:, h * P:(h + 1) * P], ident[:])
                last.then_inc(ck_T, 1)
        pe.wait_ge(ct0_ready, 1)
        pe.wait_ge(ck_ready, 1)
        for g, (d, t) in enumerate(MG):
            tok = slice(t * P, (t + 1) * P)
            unit_a = ALONE * NT + 2 * g
            proj(unit_a, 0)
            pe.wait_ge(mdiag_ready, g + 1)
            if g >= 1:
                pe.wait_ge(w_ready, g)
            mm(PS[:, 5, :], identb[:], masksb[:, d, :].unsqueeze(1).broadcast_to([P, H, P]), start=True, stop=False)
            mm(PS[:, 5, :], ones4[:], mdiag.rearrange("p h t -> p (h t)"), start=False, stop=True).then_inc(mb_done, 1)
            if g >= 1:
                pe.wait_ge(sw_ready, g)
            if 1 <= g <= 2:
                pe.wait_ge(newC_ready, g)
            for h in range(H):
                last = mm(PS[:, 4, h * P:(h + 1) * P], mkT[:, h, tok], mqT[:, h, tok], start=True, stop=True)
            last.then_inc(st_done, 1)
            bank = lambda h: PS[:, 6 + h // 2, (h % 2) * 129:(h % 2 + 1) * 129]
            if g >= 1:
                pe.wait_ge(num_read, g)
            if g < NUPD:
                pe.wait_ge(kw_ready, g + 1)
                pe.wait_ge(mm_evac, ALONE * NT)
                for h in range(H):
                    last = mm(bank(h), kw[:, g % 2, h, :], mv1[:, t, h, :], start=True, stop=True)
                last.then_inc(upd_done, 1)
            if g >= 1:
                heads_T(unit_a - 1)
            proj(unit_a, 1)
            if g < NUPD:
                pe.wait_ge(ct_ready, g + 1)
            if t > 0:
                i = (g // 2) - 1
                for h in range(H):
                    last = mm(bank(h), mqT[:, h, tok], CT[:, d, i % 2, h, :], start=True, stop=True)
                last.then_inc(int_done, 1)
            proj(unit_a + 1, 0)
            if t > 0:
                pe.wait_ge(int_read, g - 1)
            pe.wait_ge(sw_ready, g + 1)
            for h in range(H):
                last = mm(bank(h), sw[:, g % 2, h, :], mv1[:, t, h, :], start=True, stop=True)
            last.then_inc(num_done, 1)
            if g < 2:
                for h in range(H):
                    last = tr(PS[:, 4, h * P:(h + 1) * P], CT[:, d, 1, h, 0:HD], ident[:])
                last.then_inc(newC_T, 1)
            proj(unit_a + 1, 1)
            heads_T(unit_a)
        pe.wait_ge(mm_evac, NT * len(WIN_ORDER))
        pe.wait_ge(win_Tevac, len(T_NO))
        pe.wait_ge(w_ready, NMG)
        pe.wait_ge(num_read, NMG)
        for u in range(NU + 4):
            if u % NT == 1 and u > 1:
                hh = u // NT - 1
                pe.wait_ge(aT_ready, NT * (hh + 1))
                if hh >= 1:
                    pe.wait_ge(omix, hh)
                for kt in range(5):
                    v = vc[:, hh, :] if kt == 4 else dv_tok[:, 1 + kt, hh, :]
                    last = mm(PS[:, 6, :], v, aT[:, hh % 2, kt, :], start=(kt == 0), stop=(kt == 4))
                last.then_inc(pv_done, 1)
                pe.wait_ge(aT_ready, u - 1 if u <= NU else NU)
                mm(PS[:, 3, P:2 * P], dv_tok[:, 0, hh, :], aTc[:, hh % 2, :], start=True, stop=True).then_inc(pvc_done, 1)
            if u < NU:
                h, j = UNITS[u]
                if u >= 1:
                    pe.wait_ge(pexp_done, 2 * u)
                for m in range(2):
                    q = dqT[QK * m:QK * m + QK, h, j * P:(j + 1) * P]
                    k_, c_ = dkT[QK * m:QK * m + QK, h], ckT[QK * m:QK * m + QK, h]
                    if j == 0:
                        last = mm(scores[:, m, 0:P], q, k_[:, 0:CTX], start=True, stop=True)
                    else:
                        if m == 1:
                            pe.wait_ge(sc_done, 2 * u + 1)
                        cut = 512 if m == 0 else 384
                        mm(scores[:, m, 0:cut], q, k_[:, CTX:CTX + cut], start=True, stop=True)
                        if cut < LAT:
                            mm(scores[:, m, cut:LAT], q, k_[:, CTX + cut:T], start=True, stop=True)
                        last = mm(scores[:, m, LAT:LAT + PAST], q, c_, start=True, stop=True)
                    last.then_inc(sc_done, 1)
            if u % NT == 2 and u > 2:
                hh = u // NT - 1
                pe.wait_ge(osq_ready, hh + 1)
                pe.wait_ge(mix_ready, NT if hh >= 1 else 1)
                mm(PS[:, 7, :], onesf[:], osq[:, CTX:T], start=True, stop=True).then_inc(oss_done, 1)
                pe.wait_ge(aT_ready, u - 1 if u <= NU else NU)
                mm(PS[:, 4, P:2 * P], onesf[:], osq[:, 0:CTX], start=True, stop=True).then_inc(ossc_done, 1)
            if u < NU and j >= 1:
                qn = 4 * h + j - 1
                n_, hf = 4 + qn // 2, qn % 2
                ci = ADA2 + n_ - 4
                if hf == 0 and n_ > 4:
                    pe.wait_ge(ada_row, n_)
                halves(ci, hf)
                for k in range(4 * hf, 4 * hf + 4):
                    last = mm(PS[0:2, 5, :], silc[:, k, :], ring[:, ci % 2, k, :], start=(k == 0), stop=(k == KD - 1))
                if hf == 1:
                    last.then_inc(ada_done, 1)
            if 1 <= u <= NU:
                j1 = UNITS[u - 1][1]
                pe.wait_ge(a_ready, u)
                if u >= 2:
                    pe.wait_ge(aT_ready, u - 1)
                if u % NT == 1 and u > 1:
                    pe.wait_ge(osq_ready, u // NT)
                if u % NT == 2 and u > 2:
                    pe.wait_ge(ossc_read, u // NT)
                for kt in range(1 if j1 == 0 else 5):
                    last = tr(aT_ps[:, kt * P:(kt + 1) * P], pexp[:, (u - 1) % 2, 0, kt * P:(kt + 1) * P], ident[:])
                last.then_inc(a_T, 1)
            if u in MIX_STEPS:
                t = MIX_STEPS.index(u)
                pe.wait_ge(hm_normed, t + 1)
                if t >= 1:
                    pe.wait_ge(mix_ready, t)
                if t == 1:
                    pe.wait_ge(orstd, 1)
                for hh in range(H):
                    last = tr(mix_bank(t)[:, hh * P:(hh + 1) * P], hm[:, t, hh, :], ident[:])
                last.then_inc(mix_T, 1)
        pe.wait_ge(mix_ready, NT)
        pe.wait_ge(omix, H)
        for hf in range(2):
            halves(WOUT, hf)
            halves(WOUT + 1, hf)
        for t in range(NT + 2):
            for q in range(2):
                if t < NT:
                    i = 2 * t + q
                    if i >= 4:
                        pe.wait_ge(x1_ready, i - 3)
                    for k in range(KD):
                        last = mm(PS[:, i % 4, :], hTv[:, k, t * P:(t + 1) * P], ring[:, (WOUT + q) % 2, k, :],
                                  start=(k == 0), stop=(k == KD - 1))
                    last.then_inc(o_done, 1)
                if q == 0 and 1 <= t <= NT:
                    tt = t - 1
                    pe.wait_ge(h2_ready, tt + 1)
                    if tt >= 1:
                        pe.wait_ge(h2T_ready, tt)
                    for k in range(KD):
                        last = tr(PS[:, 4 + k // 4, (k % 4) * P:(k % 4 + 1) * P], h2[:, tt % 2, k * P:(k + 1) * P], ident[:])
                    last.then_inc(h2_T, 1)
                if q == 0 and t >= 2:
                    pe.wait_ge(logT_read, t - 1)
                    tr(PS[:, 6, 128:148], lgT[:], ident[0:20, 0:20]).then_inc(route_done, 1)
            if 1 <= t <= NT:
                tt = t - 1
                pe.wait_ge(h2T_ready, tt + 1)
                if tt >= 1:
                    pe.wait_ge(oh_ready, tt)
                for k in range(KD):
                    last = mm(PS[0:20, 6, 0:P], wroute[:, k, :], hTv[:, k, tt * P:(tt + 1) * P],
                              start=(k == 0), stop=(k == KD - 1))
                last.then_inc(logT, 1)
            if t >= 2:
                tt = t - 2
                pe.wait_ge(oh_ready, tt + 1)
                for j in range(tt + 1):
                    last = mm(PS[:, 7, NE * tt:NE * tt + NE], masksb[:, 2 if j == tt else 3, :], ohb[:, j, :],
                              start=(j == 0), stop=(j == tt))
                if tt == NT - 1:
                    for j in range(NT):
                        last = mm(PS[:, 7, 80:96], masksb[:, 3, :], ohb[:, j, :], start=(j == 0), stop=(j == NT - 1))
                last.then_inc(rank_done, 1)
        pe.wait_ge(rounds_ready, 1)
        n_rounds = pe.value_load(rnd[0:1, 0:1], min_val=1, max_val=ROUNDS)
        for b in range(2):
            pe.sem_inc(xg_T[b], 1)
            pe.sem_inc(gu_done[b], 1)
            pe.sem_inc(dn_done[b], 1)
        with pe.Fori(0, n_rounds * PAIRS) as it:
            for b in range(2):
                pe.wait_ge(xg_in[b], 16 * it + 16)
                pe.wait_ge(yo_ready[b], it + 1)
                for k in range(KD):
                    last = tr(PS[:, 2 * b + k // 4, (k % 4) * P:(k % 4 + 1) * P], xg[:, b, k * P:(k + 1) * P], ident[:])
                last.then_inc(xg_T[b], 1)
            for b in range(2):
                pe.wait_ge(xgT_ready[b], it + 1)
                pe.wait_ge(wg_in[b], 16 * it + 16)
                pe.wait_ge(hid_ready[b], it + 1)
                for k in range(KD):
                    last = mm(PS[:, 4 + b, :], xgT[:, b, k, :], gub[b][:, k, :], start=(k == 0), stop=(k == KD - 1))
                    if b == 1 and k == 3:
                        pe.wait_ge(hid_ready[0], it + 2)
                        for b_ in range(2):
                            pe.wait_ge(hidT_ready[b_], it + 1)
                        for k_ in range(2):
                            th = tr(PS[:, 6, k_ * P:(k_ + 1) * P], hid[:, 0, k_ * P:(k_ + 1) * P], ident[:])
                        th.then_inc(hid_T[0], 1)
                last.then_inc(gu_done[b], 1)
            for b in range(2):
                pe.wait_ge(hidT_ready[b], it + 2)
                pe.wait_ge(wd_in[b], 16 * it + 16)
                for q in range(2):
                    for k in range(2):
                        last = mm(PS[:, 2 * b + q, :], hidT[:, b, k, :], dnb[b][:, k, q * 512:(q + 1) * 512],
                                  start=(k == 0), stop=(k == 1))
                    if b == 0 and q == 0:
                        pe.wait_ge(hid_ready[1], it + 2)
                        for k_ in range(2):
                            th = tr(PS[:, 6, 256 + k_ * P:256 + (k_ + 1) * P], hid[:, 1, k_ * P:(k_ + 1) * P], ident[:])
                        th.then_inc(hid_T[1], 1)
                last.then_inc(dn_done[b], 1)


_INS = ["x_prompt", "x_sample", "cache_k", "cache_v", "state_C", "state_n", "state_m", "c", "c_ctx", "w_ada", "b_ada",
        "norm_mix", "norm_ffn", "w_in", "b_gate", "mlstm_norm", "diff_norm", "diff_lambda", "w_out", "w_route_group",
        "b_route_group", "w_route_expert", "b_route_expert", "w_gate_up", "w_down", "final_norm"]
_OUTS = {"y_prompt": (1, CTX, D), "y_sample": (1, LAT, D), "new_k": (1, 1, CTX, H, 2, QK), "new_v": (1, 1, CTX, H, HD),
         "new_C": (1, 1, 2, H, HD, HD), "new_n": (1, 1, 2, H, HD), "new_m": (1, 1, 2, H)}
_SCRATCH = {"mod": ((2, 4 * D), F32), "h2": ((T, D), F32), "y": ((NE * P, D), F32), "ids": ((ROUNDS * NE * P, 1), U32)}


def kernel(**inputs):
    import concourse.bacc as _bacc
    from concourse.bass_utils import run_bass_kernel_spmd as _run

    nc = _bacc.Bacc("TRN2", target_bir_lowering=False, num_devices=1)
    arrays = {k: np.ascontiguousarray(inputs[k]) for k in _INS}
    arrays.update(shape_constants())
    a = {k: nc.dram_tensor(f"in_{k}", v.shape, mybir.dt.from_np(v.dtype), kind="ExternalInput").ap() for k, v in arrays.items()}
    o = {k: nc.dram_tensor(f"out_{k}", v, F32, kind="ExternalOutput").ap() for k, v in _OUTS.items()}
    s = {k: nc.dram_tensor(f"scratch_{k}", v, dt, kind="Internal").ap() for k, (v, dt) in _SCRATCH.items()}
    build(nc, a, o, s)
    r = _run(nc, [{f"in_{k}": v for k, v in arrays.items()}], core_ids=[0])
    return tuple(r.results[0][f"out_{k}"] for k in _OUTS)
```
